# Optimizing a Trainium2 kernel written in Bass

```python
import jax, jax.numpy as jnp
from jax import lax
import numpy as np
import math
import jax
import jax.numpy as jnp

D_MODEL = 1024
BATCH = 1
SEQ = 1024
DEPTH = 2

GRID_W = 64
CTX_LEN = 256
NORM_EPS = 1e-6
ROPE_BASE = 10000.0
Q_BLOCK = 128

MLA_HEADS = 6
MLA_Q_RANK = 256
MLA_KV_RANK = 128
MLA_NOPE = 64
MLA_ROPE = 32
MLA_V = 64
MLA_WIDTH = MLA_HEADS * MLA_V
MLA_SCALE = (MLA_NOPE + MLA_ROPE) ** -0.5

SWA_HEADS = 6
SWA_KV_HEADS = 2
SWA_REP = SWA_HEADS // SWA_KV_HEADS
SWA_HEAD_DIM = 64
SWA_WINDOW = 128
SWA_WIDTH = SWA_HEADS * SWA_HEAD_DIM
SWA_SCALE = SWA_HEAD_DIM ** -0.5

CONV_CH = 256
CONV_K = 3

MIX_WIDTH = MLA_WIDTH + SWA_WIDTH + CONV_CH
IN_SPLITS = (MLA_Q_RANK, MLA_KV_RANK, MLA_ROPE, SWA_WIDTH, SWA_KV_HEADS * SWA_HEAD_DIM, SWA_KV_HEADS * SWA_HEAD_DIM, CONV_CH, CONV_CH, CONV_CH)
IN_WIDTH = sum(IN_SPLITS)

N_EXPERTS = 16
EXPERT_FF = 512
EC_CAPACITY_FACTOR = 2
N_MOD = 6


def rmsnorm(x, g):
    xf = x.astype(jnp.float32)
    y = xf * lax.rsqrt(jnp.mean(xf * xf, axis=-1, keepdims=True) + NORM_EPS)
    return (y * g.astype(jnp.float32)).astype(x.dtype)

def axial_rope(n_tokens, rot_dim, dtype):
    rows = n_tokens // GRID_W
    row = jnp.repeat(jnp.arange(rows, dtype=jnp.float32), GRID_W)
    col = jnp.tile(jnp.arange(GRID_W, dtype=jnp.float32), rows)
    n_freq = rot_dim // 4
    inv = ROPE_BASE ** (-jnp.arange(n_freq, dtype=jnp.float32) / n_freq)
    ang = jnp.concatenate([row[:, None] * inv, col[:, None] * inv], axis=-1)
    return jnp.cos(ang).astype(dtype), jnp.sin(ang).astype(dtype)

def apply_rope(x, cos, sin):
    shape = (cos.shape[0],) + (1,) * (x.ndim - 3) + (cos.shape[1],)
    cos = cos.reshape(shape)
    sin = sin.reshape(shape)
    x1, x2 = jnp.split(x, 2, axis=-1)
    return jnp.concatenate([x1 * cos - x2 * sin, x2 * cos + x1 * sin], axis=-1)

def split_columns(p):
    offs = [int(o) for o in np.cumsum(IN_SPLITS)[:-1]]
    return jnp.split(p, offs, axis=-1)

def to_blocks(t):
    b, n = t.shape[0], t.shape[1]
    return jnp.moveaxis(t.reshape((b, n // Q_BLOCK, Q_BLOCK) + t.shape[2:]), 1, 0)

def from_blocks(o):
    nb, b, qb = o.shape[0], o.shape[1], o.shape[2]
    return jnp.moveaxis(o, 0, 1).reshape(b, nb * qb, -1)

def mla_q(p_q, q_norm_g, w_uq):
    b, t = p_q.shape[0], p_q.shape[1]
    q = (rmsnorm(p_q, q_norm_g) @ w_uq).reshape(b, t, MLA_HEADS, MLA_NOPE + MLA_ROPE)
    return q[..., :MLA_NOPE], q[..., MLA_NOPE:]

def mla_kv(p_kv, kv_norm_g, w_ukv):
    b, t = p_kv.shape[0], p_kv.shape[1]
    kv = (rmsnorm(p_kv, kv_norm_g) @ w_ukv).reshape(b, t, MLA_HEADS, MLA_NOPE + MLA_V)
    return kv[..., :MLA_NOPE], kv[..., MLA_NOPE:]

def mla_block(qn, qr, kn, kr, v):
    s = (jnp.einsum('bqhd,bkhd->bhqk', qn, kn) + jnp.einsum('bqhr,bkr->bhqk', qr, kr)).astype(jnp.float32) * MLA_SCALE
    p = jax.nn.softmax(s, axis=-1).astype(v.dtype)
    return jnp.einsum('bhqk,bkhd->bqhd', p, v)

def mla_latent(qn, qr, kn, kr, v):
    out = lax.map(lambda a: mla_block(a[0], a[1], kn, kr, v), (to_blocks(qn), to_blocks(qr)))
    return from_blocks(out)

def sink_softmax(scores, sink):
    s_sink = jnp.broadcast_to(sink.astype(jnp.float32)[None, :, :, None, None], scores.shape[:-1] + (1,))
    p = jax.nn.softmax(jnp.concatenate([scores, s_sink], axis=-1), axis=-1)
    return p[..., :-1]

def swa_latent(q, k, v, k_ctx, v_ctx, sink):
    s_len = q.shape[1]
    n_ctx = k_ctx.shape[1]
    nb = s_len // Q_BLOCK
    band = Q_BLOCK + 2 * SWA_WINDOW
    pad = ((0, 0), (SWA_WINDOW, SWA_WINDOW), (0, 0), (0, 0))
    kp = jnp.pad(k, pad)
    vp = jnp.pad(v, pad)
    q_off = jnp.arange(Q_BLOCK)
    k_off = jnp.arange(band)

    def block(args):
        i, q_b = args
        start = i * Q_BLOCK
        k_b = lax.dynamic_slice_in_dim(kp, start, band, axis=1)
        v_b = lax.dynamic_slice_in_dim(vp, start, band, axis=1)
        q_pos = start + q_off
        k_pos = start - SWA_WINDOW + k_off
        valid = (jnp.abs(q_pos[:, None] - k_pos[None, :]) <= SWA_WINDOW) & ((k_pos >= 0) & (k_pos < s_len))[None, :]
        s_loc = jnp.einsum('bqgrd,bkgd->bgrqk', q_b, k_b).astype(jnp.float32) * SWA_SCALE
        s_loc = jnp.where(valid, s_loc, -jnp.inf)
        s_ctx = jnp.einsum('bqgrd,bcgd->bgrqc', q_b, k_ctx).astype(jnp.float32) * SWA_SCALE
        p = sink_softmax(jnp.concatenate([s_ctx, s_loc], axis=-1), sink).astype(v.dtype)
        return (jnp.einsum('bgrqc,bcgd->bqgrd', p[..., :n_ctx], v_ctx)
                + jnp.einsum('bgrqk,bkgd->bqgrd', p[..., n_ctx:], v_b))

    out = lax.map(block, (jnp.arange(nb), to_blocks(q)))
    return from_blocks(out)

def swa_context(q, k, v, sink):
    s = jnp.einsum('bqgrd,bcgd->bgrqc', q, k).astype(jnp.float32) * SWA_SCALE
    p = sink_softmax(s, sink).astype(v.dtype)
    o = jnp.einsum('bgrqc,bcgd->bqgrd', p, v)
    return o.reshape(o.shape[0], o.shape[1], SWA_WIDTH)

def short_conv(b_gate, c_gate, u, w):
    z = c_gate * u
    y = lax.conv_general_dilated(z, w[:, None, :].astype(z.dtype), window_strides=(1,),
                                 padding=((CONV_K // 2, CONV_K // 2),),
                                 dimension_numbers=('NWC', 'WIO', 'NWC'),
                                 feature_group_count=CONV_CH)
    return b_gate * y

def ec_ffn(h, router_w, w_gate, w_up, w_down):
    n_tok, d = h.shape[1], h.shape[2]
    cap = EC_CAPACITY_FACTOR * n_tok // N_EXPERTS
    aff = jax.nn.softmax((h @ router_w).astype(jnp.float32), axis=-1)
    top_aff, idx = lax.top_k(jnp.swapaxes(aff, 1, 2), cap)
    xg = jax.vmap(lambda hb, ib: hb[ib])(h, idx)
    hid = jax.nn.silu(jnp.einsum('becd,edf->becf', xg, w_gate)) * jnp.einsum('becd,edf->becf', xg, w_up)
    y = jnp.einsum('becf,efd->becd', hid, w_down) * top_aff[..., None].astype(h.dtype)
    return jax.vmap(lambda yb, ib: jnp.zeros((n_tok, d), yb.dtype).at[ib.reshape(-1)].add(yb.reshape(-1, d)))(y, idx)

def hybrid_layer(xl, xc, c, c_ctx, ada_w, ada_b, norm1_g, w_in, q_norm_g, w_uq, kv_norm_g, w_ukv,
                 sink, conv_w, w_o, norm2_g, router_w, w_gate, w_up, w_down, rope_mla, rope_swa, update_ctx):
    b, s_len = xl.shape[0], xl.shape[1]
    n_ctx = xc.shape[1]
    sh1, sc1, g1, sh2, sc2, g2 = jnp.split((jax.nn.silu(c) @ ada_w + ada_b)[:, None, :], N_MOD, axis=-1)
    csh1, csc1, cg1, csh2, csc2, cg2 = jnp.split(jax.nn.silu(c_ctx) @ ada_w + ada_b, N_MOD, axis=-1)

    hl = rmsnorm(xl, norm1_g) * (1 + sc1) + sh1
    hc = rmsnorm(xc, norm1_g) * (1 + csc1) + csh1
    l_cq, l_ckv, l_kr, l_q, l_k, l_v, l_b, l_c, l_u = split_columns(hl @ w_in)
    c_cq, c_ckv, c_kr, c_q, c_k, c_v, c_b, c_c, c_u = split_columns(hc @ w_in)

    qn_l, qr_l = mla_q(l_cq, q_norm_g, w_uq)
    qr_l = apply_rope(qr_l, *rope_mla)
    kn_l, va_l = mla_kv(l_ckv, kv_norm_g, w_ukv)
    kr_l = apply_rope(l_kr, *rope_mla)
    kn_c, va_c = mla_kv(c_ckv, kv_norm_g, w_ukv)
    a_l = mla_latent(qn_l, qr_l, jnp.concatenate([kn_c, kn_l], axis=1),
                     jnp.concatenate([c_kr, kr_l], axis=1), jnp.concatenate([va_c, va_l], axis=1))

    sink_gr = sink.reshape(SWA_KV_HEADS, SWA_REP)
    q_l = apply_rope(l_q.reshape(b, s_len, SWA_KV_HEADS, SWA_REP, SWA_HEAD_DIM), *rope_swa)
    k_l = apply_rope(l_k.reshape(b, s_len, SWA_KV_HEADS, SWA_HEAD_DIM), *rope_swa)
    v_l = l_v.reshape(b, s_len, SWA_KV_HEADS, SWA_HEAD_DIM)
    k_c = c_k.reshape(b, n_ctx, SWA_KV_HEADS, SWA_HEAD_DIM)
    v_c = c_v.reshape(b, n_ctx, SWA_KV_HEADS, SWA_HEAD_DIM)
    b_l = swa_latent(q_l, k_l, v_l, k_c, v_c, sink_gr)

    cv_l = short_conv(l_b, l_c, l_u, conv_w)

    xl = xl + g1 * (jnp.concatenate([a_l, b_l, cv_l], axis=-1) @ w_o)
    xl = xl + g2 * ec_ffn(rmsnorm(xl, norm2_g) * (1 + sc2) + sh2, router_w, w_gate, w_up, w_down)

    if update_ctx:
        qn_c, qr_c = mla_q(c_cq, q_norm_g, w_uq)
        a_c = mla_block(qn_c, qr_c, kn_c, c_kr, va_c).reshape(b, n_ctx, MLA_WIDTH)
        b_c = swa_context(c_q.reshape(b, n_ctx, SWA_KV_HEADS, SWA_REP, SWA_HEAD_DIM), k_c, v_c, sink_gr)
        cv_c = short_conv(c_b, c_c, c_u, conv_w)
        xc = xc + cg1 * (jnp.concatenate([a_c, b_c, cv_c], axis=-1) @ w_o)
        xc = xc + cg2 * ec_ffn(rmsnorm(xc, norm2_g) * (1 + csc2) + csh2, router_w, w_gate, w_up, w_down)
    return xl, xc

def first_inputs(seed: int = 0) -> dict:
    key = jax.random.key(seed)
    ks = jax.random.split(key, 21)
    f32 = jnp.float32
    D = D_MODEL

    def nrm(k, shape, scale):
        return jax.random.normal(k, shape, f32) * scale

    def gain(k, shape):
        return 1.0 + 0.02 * jax.random.normal(k, shape, f32)

    return {
        'x': nrm(ks[0], (BATCH, SEQ, D), 1.0),
        'c': nrm(ks[1], (BATCH, D), 1.0),
        'ctx': nrm(ks[2], (BATCH, CTX_LEN, D), 1.0),
        'c_ctx': nrm(ks[3], (D,), 1.0),
        'ada_w': nrm(ks[4], (DEPTH, D, N_MOD * D), 0.5 * D ** -0.5),
        'ada_b': nrm(ks[5], (DEPTH, N_MOD * D), 0.02),
        'norm1_g': gain(ks[6], (DEPTH, D)),
        'w_in': nrm(ks[7], (DEPTH, D, IN_WIDTH), D ** -0.5),
        'mla_q_norm_g': gain(ks[8], (DEPTH, MLA_Q_RANK)),
        'mla_w_uq': nrm(ks[9], (DEPTH, MLA_Q_RANK, MLA_HEADS * (MLA_NOPE + MLA_ROPE)), MLA_Q_RANK ** -0.5),
        'mla_kv_norm_g': gain(ks[10], (DEPTH, MLA_KV_RANK)),
        'mla_w_ukv': nrm(ks[11], (DEPTH, MLA_KV_RANK, MLA_HEADS * (MLA_NOPE + MLA_V)), MLA_KV_RANK ** -0.5),
        'swa_sink': nrm(ks[12], (DEPTH, SWA_HEADS), 0.5),
        'conv_w': nrm(ks[13], (DEPTH, CONV_K, CONV_CH), CONV_K ** -0.5),
        'w_o': nrm(ks[14], (DEPTH, MIX_WIDTH, D), MIX_WIDTH ** -0.5),
        'norm2_g': gain(ks[15], (DEPTH, D)),
        'router_w': nrm(ks[16], (DEPTH, D, N_EXPERTS), D ** -0.5),
        'exp_w_gate': nrm(ks[17], (DEPTH, N_EXPERTS, D, EXPERT_FF), D ** -0.5),
        'exp_w_up': nrm(ks[18], (DEPTH, N_EXPERTS, D, EXPERT_FF), D ** -0.5),
        'exp_w_down': nrm(ks[19], (DEPTH, N_EXPERTS, EXPERT_FF, D), EXPERT_FF ** -0.5),
        'final_norm_g': gain(ks[20], (D,)),
    }

def first_block(x, c, ctx, c_ctx, ada_w, ada_b, norm1_g, w_in, mla_q_norm_g, mla_w_uq, mla_kv_norm_g,
              mla_w_ukv, swa_sink, conv_w, w_o, norm2_g, router_w, exp_w_gate, exp_w_up, exp_w_down,
              final_norm_g):
    n_lat = x.shape[1]
    rope_mla = axial_rope(n_lat, MLA_ROPE, x.dtype)
    rope_swa = axial_rope(n_lat, SWA_HEAD_DIM, x.dtype)
    xl, xc = x, ctx
    for li in range(DEPTH):
        xl, xc = hybrid_layer(xl, xc, c, c_ctx, ada_w[li], ada_b[li], norm1_g[li], w_in[li],
                              mla_q_norm_g[li], mla_w_uq[li], mla_kv_norm_g[li], mla_w_ukv[li],
                              swa_sink[li], conv_w[li], w_o[li], norm2_g[li], router_w[li],
                              exp_w_gate[li], exp_w_up[li], exp_w_down[li], rope_mla, rope_swa,
                              li < DEPTH - 1)
    return rmsnorm(xl, final_norm_g)


DEPTH_2 = 1

HEAD_DIM = 64
ROPE_THETA = 10000.0
F32 = jnp.float32

A_HEADS = 4
A_QK = HEAD_DIM
A_V = 2 * HEAD_DIM
A_QBLOCK = 128
B_HEADS = 4
B_DK = HEAD_DIM // 2
B_DV = HEAD_DIM
B_GATE_RANK = 16
B_GATE_TAU = 16.0
B_CHUNK = 64
C_HEADS = 4
C_DH = HEAD_DIM
NA_ROWS = 8
NA_COLS = 16

A_WIDTH = A_HEADS * A_V
B_WIDTH = B_HEADS * B_DV
C_WIDTH = C_HEADS * C_DH
MIX_WIDTH_2 = A_WIDTH + B_WIDTH + C_WIDTH

IN_SIZES = (A_HEADS * 2 * A_QK, A_HEADS * 2 * A_QK, A_WIDTH,
            B_HEADS * B_DK, B_HEADS * B_DK, B_WIDTH, B_WIDTH, 2 * B_GATE_RANK,
            C_WIDTH, C_WIDTH, C_WIDTH)
IN_WIDTH_2 = sum(IN_SIZES)

N_GROUPS = 4
EXPERTS_PER_GROUP = 8
N_EXPERTS_2 = N_GROUPS * EXPERTS_PER_GROUP
TOP_K = 2
EXPERT_HIDDEN = 512
MOE_BLOCK = 128


def rms_norm(x, g):
    xf = x.astype(F32)
    y = xf * lax.rsqrt(jnp.mean(xf * xf, axis=-1, keepdims=True) + NORM_EPS)
    return (y * g.astype(F32)).astype(x.dtype)

def split_in(p):
    return jnp.split(p, np.cumsum(IN_SIZES)[:-1].tolist(), axis=-1)

def axial_rope_tables(n_tokens, dtype):
    t = jnp.arange(n_tokens)
    row = (t // GRID_W).astype(F32)
    col = (t % GRID_W).astype(F32)
    n_freq = HEAD_DIM // 4
    inv = ROPE_THETA ** (-jnp.arange(n_freq, dtype=F32) / n_freq)
    ang_r = row[:, None] * inv
    ang_c = col[:, None] * inv
    return (jnp.cos(ang_r).astype(dtype), jnp.sin(ang_r).astype(dtype),
            jnp.cos(ang_c).astype(dtype), jnp.sin(ang_c).astype(dtype))

def apply_axial_rope(x, tabs):
    cr, sr, cc, sc = (tb.reshape((tb.shape[0],) + (1,) * (x.ndim - 3) + (tb.shape[1],)) for tb in tabs)
    x1, x2, x3, x4 = jnp.split(x, 4, axis=-1)
    return jnp.concatenate([x1 * cr - x2 * sr, x2 * cr + x1 * sr,
                            x3 * cc - x4 * sc, x4 * cc + x3 * sc], axis=-1)

def diff_attention(q, k, v, qc, kc, vc, lam, lam_init, g_sub, need_ctx):
    B_, S = q.shape[:2]
    L = qc.shape[1]
    scale = A_QK ** -0.5
    k_all = jnp.concatenate([kc, k], axis=1)
    v_all = jnp.concatenate([vc, v], axis=1)

    def attend(qb, kb, vb):
        s = jnp.einsum('bqhmd,bkhmd->bhmqk', qb, kb).astype(F32) * scale
        p = jax.nn.softmax(s, axis=-1)
        d = p[:, :, 0] - lam * p[:, :, 1]
        return jnp.einsum('bhqk,bkhv->bqhv', d.astype(vb.dtype), vb)

    nb = S // A_QBLOCK
    qblocks = jnp.moveaxis(q.reshape((B_, nb, A_QBLOCK) + q.shape[2:]), 1, 0)
    o = lax.map(lambda qb: attend(qb, k_all, v_all), qblocks)
    o = jnp.moveaxis(o, 0, 1).reshape(B_, S, A_HEADS, A_V)
    out = (rms_norm(o, g_sub) * (1.0 - lam_init)).reshape(B_, S, A_WIDTH)
    out_c = None
    if need_ctx:
        oc = attend(qc, kc, vc)
        out_c = (rms_norm(oc, g_sub) * (1.0 - lam_init)).reshape(B_, L, A_WIDTH)
    return out, out_c

def gla_scan(q, k, v, log_a, s0):
    B_, H, T, dk = q.shape
    n = T // B_CHUNK

    def chunks(t):
        return jnp.moveaxis(t.reshape(B_, H, n, B_CHUNK, t.shape[-1]), 2, 0)

    causal = jnp.tril(jnp.ones((B_CHUNK, B_CHUNK), dtype=bool))

    def step(s, inp):
        qc, kc, vc, ac = inp
        b = jnp.cumsum(ac, axis=2)
        rel = jnp.where(causal[:, :, None], b[:, :, :, None, :] - b[:, :, None, :, :], -jnp.inf)
        a_intra = jnp.einsum('bhtsd,bhsd->bhts', qc[:, :, :, None, :] * jnp.exp(rel), kc)
        o = (jnp.einsum('bhts,bhsv->bhtv', a_intra, vc)
             + jnp.einsum('bhtd,bhdv->bhtv', qc * jnp.exp(b), s))
        b_end = b[:, :, -1, :]
        s = (jnp.exp(b_end)[..., None] * s
             + jnp.einsum('bhsd,bhsv->bhdv', kc * jnp.exp(b_end[:, :, None, :] - b), vc))
        return s, o

    s_final, o = lax.scan(step, s0, (chunks(q), chunks(k), chunks(v), chunks(log_a)))
    o = jnp.moveaxis(o, 0, 2).reshape(B_, H, T, v.shape[-1])
    return o, s_final

def gla_mixer(q, k, v, r, glow, qc, kc, vc, rc, glowc, w_dec, b_dec, g_out, need_ctx):
    B_ = q.shape[0]

    def heads(t, d):
        return jnp.transpose(t.reshape(t.shape[0], t.shape[1], -1, d), (0, 2, 1, 3)).astype(F32)

    def decay(gl, direction):
        z = gl[..., direction * B_GATE_RANK:(direction + 1) * B_GATE_RANK] @ w_dec[direction] + b_dec[direction]
        return heads(jax.nn.log_sigmoid(z.astype(F32)) / B_GATE_TAU, B_DK)

    def flip(t):
        return jnp.flip(t, axis=2)

    scale = B_DK ** -0.5
    ql, kl, vl = heads(q, B_DK) * scale, heads(k, B_DK), heads(v, B_DV)
    qx, kx, vx = heads(qc, B_DK) * scale, heads(kc, B_DK), heads(vc, B_DV)
    s0 = jnp.zeros((B_, B_HEADS, B_DK, B_DV), F32)
    ox_f, sx_f = gla_scan(qx, kx, vx, decay(glowc, 0), s0)
    ol_f, _ = gla_scan(ql, kl, vl, decay(glow, 0), sx_f)
    ox_b, sx_b = gla_scan(flip(qx), flip(kx), flip(vx), flip(decay(glowc, 1)), s0)
    ol_b, _ = gla_scan(flip(ql), flip(kl), flip(vl), flip(decay(glow, 1)), sx_b)

    def readout(o, gate):
        o = jnp.transpose(rms_norm(o, g_out), (0, 2, 1, 3)).reshape(gate.shape[0], gate.shape[1], B_WIDTH)
        return (o * jax.nn.silu(gate.astype(F32))).astype(gate.dtype)

    out = readout(ol_f + flip(ol_b), r)
    out_c = readout(ox_f + flip(ox_b), rc) if need_ctx else None
    return out, out_c

def neighborhood_attention(q, k, v, qc, kc, vc, rpb, need_ctx):
    B_, S, H, dh = q.shape
    L = qc.shape[1]
    rows = S // GRID_W
    wr = min(NA_ROWS, rows)
    scale = dh ** -0.5

    def grid(t):
        return jnp.transpose(t.reshape(B_, rows, GRID_W, H, dh), (0, 3, 1, 2, 4))

    qg, kg, vg = grid(q), grid(k), grid(v)
    r = jnp.arange(rows)
    row_idx = jnp.clip(r - wr // 2, 0, rows - wr)[:, None] + jnp.arange(wr)
    cq = jnp.arange(GRID_W)
    col_start = jnp.clip(cq - NA_COLS // 2, 0, GRID_W - NA_COLS)
    col_mask = (cq[None, :] >= col_start[:, None]) & (cq[None, :] < col_start[:, None] + NA_COLS)
    k_rows = kg[:, :, row_idx]
    v_rows = vg[:, :, row_idx]
    s_nb = jnp.einsum('bhrqd,bhrwkd->bhrqwk', qg, k_rows).astype(F32) * scale
    dr = row_idx - r[:, None] + (NA_ROWS - 1)
    dc = jnp.clip(cq[None, :] - cq[:, None], -(NA_COLS - 1), NA_COLS - 1) + (NA_COLS - 1)
    bias = rpb[:, dr[:, None, :, None], dc[None, :, None, :]].astype(F32)
    s_nb = jnp.where(col_mask[:, None, :], s_nb + bias, -jnp.inf)
    s_c = jnp.einsum('bhrqd,bchd->bhrqc', qg, kc).astype(F32) * scale
    n_nb = wr * GRID_W
    p = jax.nn.softmax(jnp.concatenate([s_nb.reshape(B_, H, rows, GRID_W, n_nb), s_c], axis=-1), axis=-1)
    p_nb = p[..., :n_nb].reshape(s_nb.shape).astype(v.dtype)
    p_c = p[..., n_nb:].astype(v.dtype)
    o = (jnp.einsum('bhrqwk,bhrwkd->bhrqd', p_nb, v_rows)
         + jnp.einsum('bhrqc,bchd->bhrqd', p_c, vc))
    out = jnp.transpose(o, (0, 2, 3, 1, 4)).reshape(B_, S, H * dh)
    out_c = None
    if need_ctx:
        sc = jnp.einsum('bqhd,bkhd->bhqk', qc, kc).astype(F32) * scale
        out_c = jnp.einsum('bhqk,bkhd->bqhd', jax.nn.softmax(sc, axis=-1).astype(vc.dtype), vc).reshape(B_, L, H * dh)
    return out, out_c

def hier_moe(h, w_rg, b_rg, w_re, b_re, w_up, w_down):
    n_tok, D = h.shape
    n_assign = n_tok * TOP_K
    n_blocks = -(-(n_assign + N_EXPERTS_2 * (MOE_BLOCK - 1)) // MOE_BLOCK)
    logit_g = (h @ w_rg + b_rg).astype(F32)
    grp = jnp.argmax(logit_g, axis=-1)
    p_grp = jnp.take_along_axis(jax.nn.softmax(logit_g, axis=-1), grp[:, None], axis=1)
    logit_e = (h @ w_re + b_re).astype(F32).reshape(n_tok, N_GROUPS, EXPERTS_PER_GROUP)
    logit_e = jnp.take_along_axis(logit_e, grp[:, None, None], axis=1)[:, 0]
    top_v, top_i = lax.top_k(logit_e, TOP_K)
    gate = jax.nn.softmax(top_v, axis=-1) * p_grp
    expert = (grp[:, None] * EXPERTS_PER_GROUP + top_i).reshape(-1)
    order = jnp.argsort(expert)
    e_sorted = expert[order]
    tok_sorted = order // TOP_K
    counts = jnp.bincount(expert, length=N_EXPERTS_2)
    padded = (counts + MOE_BLOCK - 1) // MOE_BLOCK * MOE_BLOCK
    start = jnp.cumsum(counts) - counts
    pad_end = jnp.cumsum(padded)
    pad_start = pad_end - padded
    dest = pad_start[e_sorted] + jnp.arange(n_assign) - start[e_sorted]
    buf = jnp.zeros((n_blocks * MOE_BLOCK, D), h.dtype).at[dest].set(h[tok_sorted])
    blk_expert = jnp.minimum(jnp.searchsorted(pad_end, jnp.arange(n_blocks) * MOE_BLOCK, side='right'), N_EXPERTS_2 - 1)

    def expert_block(args):
        xb, e = args
        g, u = jnp.split(xb @ w_up[e], 2, axis=-1)
        return (jax.nn.silu(g) * u) @ w_down[e]

    y = lax.map(expert_block, (buf.reshape(n_blocks, MOE_BLOCK, D), blk_expert)).reshape(-1, D)
    y = y[dest] * gate.reshape(-1)[order][:, None].astype(h.dtype)
    return jax.ops.segment_sum(y, tok_sorted, num_segments=n_tok)

def hybrid_layer_2(x, xc, c_act, cc_act, rope, layer_idx, need_ctx,
                 w_mod, b_mod, g1, g2, w_in, w_out, lam, g_sub,
                 w_dec, b_dec, g_gla, rpb, w_rg, b_rg, w_re, b_re, w_up, w_down):
    B_, S, D = x.shape
    L = xc.shape[1]
    mod = (c_act @ w_mod + b_mod).reshape(B_, 6, 1, D)
    modc = (cc_act @ w_mod + b_mod).reshape(6, D)
    h = rms_norm(x, g1) * (1 + mod[:, 1]) + mod[:, 0]
    hc = rms_norm(xc, g1) * (1 + modc[1]) + modc[0]
    qa, ka, va, qb, kb, vb, rb, gb, qn, kn, vn = split_in(h @ w_in)
    qa_c, ka_c, va_c, qb_c, kb_c, vb_c, rb_c, gb_c, qn_c, kn_c, vn_c = split_in(hc @ w_in)

    lam_init = 0.8 - 0.6 * math.exp(-0.3 * layer_idx)
    lam_f = lam.astype(F32)
    lam_val = jnp.exp(jnp.sum(lam_f[0] * lam_f[1])) - jnp.exp(jnp.sum(lam_f[2] * lam_f[3])) + lam_init

    def a_qk(t):
        return t.reshape(t.shape[0], t.shape[1], A_HEADS, 2, A_QK)

    ya, ya_c = diff_attention(apply_axial_rope(a_qk(qa), rope), apply_axial_rope(a_qk(ka), rope),
                              va.reshape(B_, S, A_HEADS, A_V), a_qk(qa_c), a_qk(ka_c),
                              va_c.reshape(B_, L, A_HEADS, A_V), lam_val, lam_init, g_sub, need_ctx)
    yb, yb_c = gla_mixer(qb, kb, vb, rb, gb, qb_c, kb_c, vb_c, rb_c, gb_c, w_dec, b_dec, g_gla, need_ctx)

    def c_heads(t):
        return t.reshape(t.shape[0], t.shape[1], C_HEADS, C_DH)

    yn, yn_c = neighborhood_attention(c_heads(qn), c_heads(kn), c_heads(vn),
                                      c_heads(qn_c), c_heads(kn_c), c_heads(vn_c), rpb, need_ctx)
    x = x + mod[:, 2] * (jnp.concatenate([ya, yb, yn], axis=-1) @ w_out)
    h2 = rms_norm(x, g2) * (1 + mod[:, 4]) + mod[:, 3]
    if need_ctx:
        xc = xc + modc[2] * (jnp.concatenate([ya_c, yb_c, yn_c], axis=-1) @ w_out)
        h2c = rms_norm(xc, g2) * (1 + modc[4]) + modc[3]
        f = hier_moe(jnp.concatenate([h2.reshape(-1, D), h2c.reshape(-1, D)], axis=0),
                     w_rg, b_rg, w_re, b_re, w_up, w_down)
        x = x + mod[:, 5] * f[:B_ * S].reshape(B_, S, D)
        xc = xc + modc[5] * f[B_ * S:].reshape(B_, L, D)
    else:
        f = hier_moe(h2.reshape(-1, D), w_rg, b_rg, w_re, b_re, w_up, w_down)
        x = x + mod[:, 5] * f.reshape(B_, S, D)
    return x, xc

def second_inputs(seed: int = 0) -> dict:
    key = jax.random.key(seed)
    ks = jax.random.split(key, 23)
    D = D_MODEL

    def nrm(k, shape, s):
        return jax.random.normal(k, shape, F32) * s

    return {
        'x': nrm(ks[0], (BATCH, SEQ, D), 1.0),
        'c': nrm(ks[1], (BATCH, D), 1.0),
        'ctx': nrm(ks[2], (BATCH, CTX_LEN, D), 1.0),
        'c_ctx': nrm(ks[3], (D,), 1.0),
        'w_mod': nrm(ks[4], (DEPTH_2, D, 6 * D), 0.5 * D ** -0.5),
        'b_mod': nrm(ks[5], (DEPTH_2, 6 * D), 0.02),
        'norm1_g': 1.0 + nrm(ks[6], (DEPTH_2, D), 0.02),
        'norm2_g': 1.0 + nrm(ks[7], (DEPTH_2, D), 0.02),
        'w_in': nrm(ks[8], (DEPTH_2, D, IN_WIDTH_2), D ** -0.5),
        'w_out': nrm(ks[9], (DEPTH_2, MIX_WIDTH_2, D), MIX_WIDTH_2 ** -0.5),
        'diff_lambda': nrm(ks[10], (DEPTH_2, 4, A_QK), 0.1),
        'diff_sub_g': 1.0 + nrm(ks[11], (DEPTH_2, A_V), 0.02),
        'gla_w_decay': nrm(ks[12], (DEPTH_2, 2, B_GATE_RANK, B_HEADS * B_DK), B_GATE_RANK ** -0.5),
        'gla_b_decay': nrm(ks[13], (DEPTH_2, 2, B_HEADS * B_DK), 0.1),
        'gla_norm_g': 1.0 + nrm(ks[14], (DEPTH_2, B_DV), 0.02),
        'na_rel_bias': nrm(ks[15], (DEPTH_2, C_HEADS, 2 * NA_ROWS - 1, 2 * NA_COLS - 1), 0.02),
        'w_router_group': nrm(ks[16], (DEPTH_2, D, N_GROUPS), D ** -0.5),
        'b_router_group': nrm(ks[17], (DEPTH_2, N_GROUPS), 0.01),
        'w_router_expert': nrm(ks[18], (DEPTH_2, D, N_EXPERTS_2), D ** -0.5),
        'b_router_expert': nrm(ks[19], (DEPTH_2, N_EXPERTS_2), 0.01),
        'w_expert_up': nrm(ks[20], (DEPTH_2, N_EXPERTS_2, D, 2 * EXPERT_HIDDEN), D ** -0.5),
        'w_expert_down': nrm(ks[21], (DEPTH_2, N_EXPERTS_2, EXPERT_HIDDEN, D), EXPERT_HIDDEN ** -0.5),
        'final_g': 1.0 + nrm(ks[22], (D,), 0.02),
    }

def second_block(x, c, ctx, c_ctx, w_mod, b_mod, norm1_g, norm2_g, w_in, w_out,
              diff_lambda, diff_sub_g, gla_w_decay, gla_b_decay, gla_norm_g, na_rel_bias,
              w_router_group, b_router_group, w_router_expert, b_router_expert,
              w_expert_up, w_expert_down, final_g):
    rope = axial_rope_tables(x.shape[1], x.dtype)
    c_act = jax.nn.silu(c)
    cc_act = jax.nn.silu(c_ctx)
    xc = ctx
    for l in range(DEPTH_2):
        x, xc = hybrid_layer_2(x, xc, c_act, cc_act, rope, l, l < DEPTH_2 - 1,
                             w_mod[l], b_mod[l], norm1_g[l], norm2_g[l], w_in[l], w_out[l],
                             diff_lambda[l], diff_sub_g[l], gla_w_decay[l], gla_b_decay[l],
                             gla_norm_g[l], na_rel_bias[l], w_router_group[l], b_router_group[l],
                             w_router_expert[l], b_router_expert[l], w_expert_up[l], w_expert_down[l])
    return rms_norm(x, final_g)


def setup_inputs(seed=0):
    out = dict(first_inputs(seed))
    for name, value in second_inputs(seed + 1).items():
        if name != "x":
            out[name + "_2"] = value
    return out


def reference(
    x, c, ctx, c_ctx, ada_w, ada_b, norm1_g, w_in, mla_q_norm_g, mla_w_uq, mla_kv_norm_g,
    mla_w_ukv, swa_sink, conv_w, w_o, norm2_g, router_w, exp_w_gate, exp_w_up, exp_w_down,
    final_norm_g, c_2, ctx_2, c_ctx_2, w_mod_2, b_mod_2, norm1_g_2, norm2_g_2, w_in_2, w_out_2,
    diff_lambda_2, diff_sub_g_2, gla_w_decay_2, gla_b_decay_2, gla_norm_g_2, na_rel_bias_2,
    w_router_group_2, b_router_group_2, w_router_expert_2, b_router_expert_2, w_expert_up_2,
    w_expert_down_2, final_g_2,
):
    x = first_block(
        x, c, ctx, c_ctx, ada_w, ada_b, norm1_g, w_in, mla_q_norm_g, mla_w_uq, mla_kv_norm_g,
        mla_w_ukv, swa_sink, conv_w, w_o, norm2_g, router_w, exp_w_gate, exp_w_up, exp_w_down,
        final_norm_g,
    )
    return second_block(
        x, c_2, ctx_2, c_ctx_2, w_mod_2, b_mod_2, norm1_g_2, norm2_g_2, w_in_2, w_out_2,
        diff_lambda_2, diff_sub_g_2, gla_w_decay_2, gla_b_decay_2, gla_norm_g_2, na_rel_bias_2,
        w_router_group_2, b_router_group_2, w_router_expert_2, b_router_expert_2, w_expert_up_2,
        w_expert_down_2, final_g_2,
    )


_drawn_inputs = setup_inputs


def setup_inputs(seed=0):
    import zlib

    import numpy as np

    out = dict(_drawn_inputs(seed))
    spreads = {}
    factors = {'norm1_g': 4.068,
     'mla_q_norm_g': 8.0,
     'mla_kv_norm_g': 8.0,
     'swa_sink': 8.0,
     'norm2_g': 4.836,
     'norm1_g_2': 7.752,
     'norm2_g_2': 4.635,
     'diff_lambda_2': 3.752,
     'diff_sub_g_2': 8.0,
     'gla_w_decay_2': 3.201,
     'gla_b_decay_2': 7.338,
     'gla_norm_g_2': 8.0,
     'na_rel_bias_2': 64.0,
     'b_router_group_2': 7.837,
     'b_router_expert_2': 8.0,
     'final_g_2': 8.946}
    for name, (base, spread) in spreads.items():
        noise = np.random.default_rng([zlib.crc32(name.encode()), seed]).standard_normal(out[name].shape)
        drawn = base * np.exp(spread * noise) if base else spread * noise
        out[name] = jnp.asarray(drawn.astype(out[name].dtype))
    for name, factor in factors.items():
        out[name] = (out[name] * factor).astype(out[name].dtype)
    return out
```

```python
import concourse.bass as bass
from concourse import mybir
from contextlib import ExitStack

fp32 = mybir.dt.float32
i32 = mybir.dt.int32
u32 = mybir.dt.uint32
ALU = mybir.AluOpType
ACT = mybir.ActivationFunctionType
AX = mybir.AxisListType

D = 1024
KD = D // 128
CTX = 256
SEQ = 1024
ROWS = CTX + SEQ
TILES = ROWS // 128
CTX_TILES = CTX // 128
LAT_TILES = SEQ // 128
EPS = 1e-6
NEG = -1e30


START = 1


class Stage:

    def __init__(self, nc, name):
        self.nc, self.name, self.ctx, self.sems = nc, name, ExitStack(), []
        self.from_zero = []

    def __enter__(self):
        self.ctx.__enter__()
        return self

    def sb(self, name, shape, dt=fp32):
        return self.ctx.enter_context(self.nc.sbuf_tensor(f"{self.name}_{name}", shape, dt))

    def ps(self, name, shape, dt=fp32):
        return self.ctx.enter_context(self.nc.psum_tensor(f"{self.name}_{name}", shape, dt))

    def open(self, sp):
        for s in self.sems:
            if s not in self.from_zero:
                sp.sem_inc(s, START)

    def sem(self, name, from_zero=False):
        s = self.nc.alloc_semaphore(f"{self.name}_{name}")
        self.sems.append(s)
        if from_zero:
            self.from_zero.append(s)
        return s

    def __exit__(self, *a):
        if a[0] is None:
            nc = self.nc
            nums = sorted(s.num for s in self.sems)
            nc.clear_and_free_semaphores(self.sems)
            nc.all_engine_barrier()
        return self.ctx.__exit__(*a)


def wait_alone(eng, sem, value, passed):
    eng.wait_ge(sem, value)
    eng.sem_inc(passed, 1)


def dram_view(handle, offset, pattern):
    return bass.AP(handle, offset, [list(p) for p in pattern])


def modulation(nc, name, c, c_ctx, w, b, gain1, gain2, cols, gates, identity, beside=None):
    CH = 512
    NCH = 6 * D // CH
    with Stage(nc, name) as st:
        sb, ps, sem = st.sb, st.ps, st.sem
        cc = sb("cc", [128, KD, 2])
        ex = sb("ex", [128, KD, 2])
        sl = sb("sl", [128, KD, 2])
        bias = sb("bias", [2, 6 * D])
        gain = sb("gain", [128, 2, KD])
        row = sb("row", [2, 6 * D])
        wt = [sb(f"wt{j}", [128, KD, CH]) for j in range(2)]
        acc = [ps(f"acc{j}", [128, CH]) for j in range(2)]
        colT = ps("colT", [128, 48, 2])
        colS = sb("colS", [128, 48, 2])
        c_in, w_in0, w_in1 = sem("c_in"), sem("w_in0"), sem("w_in1")
        w_in = [w_in0, w_in1]
        e_done, s_done, row_ready = sem("e_done"), sem("s_done"), sem("row_ready")
        acc_ready = [sem("acc_ready0"), sem("acc_ready1")]
        passed_sp, passed_ve = sem("passed_sp"), sem("passed_ve")
        cols_turned, cols_copied, out_done, chain = sem("cols_turned"), sem("cols_copied"), sem("out_done"), sem("chain")
        wv = w.rearrange("(k p) n -> p k n", p=128)
        on_scalar, on_gpsimd = beside(st) if beside else (None, None)
        with nc.Block() as block:
            @block.sync
            def _(sp):
                st.open(sp)
                sp.dma_start(cc[:, :, 0], c.rearrange("(k p) -> p k", p=128), allow_slow_non_contiguous=True).then_inc(c_in, 16)
                sp.dma_start(cc[:, :, 1], c_ctx.rearrange("(k p) -> p k", p=128), allow_slow_non_contiguous=True).then_inc(c_in, 16)
                sp.dma_start(gain[:, 0, :], gain1.rearrange("(k p) -> p k", p=128), allow_slow_non_contiguous=True).then_inc(c_in, 16)
                sp.dma_start(gain[:, 1, :], gain2.rearrange("(k p) -> p k", p=128), allow_slow_non_contiguous=True).then_inc(c_in, 16)
                sp.dma_start(bias[:, :], b.partition_broadcast(2)).then_inc(c_in, 16)
                with sp.Fori(0, NCH // 2) as i:
                    for j in range(2):
                        wait_alone(sp, acc_ready[j], START + i, passed_sp)
                        sp.dma_start(wt[j][:, :, :], wv[:, :, bass.ds((i * 2 + j) * CH, CH)]).then_inc(w_in[j], 16)
                sp.wait_ge(row_ready, START + NCH)
                sp.dma_start(gates, row[:, :]).then_inc(out_done, 16)
                sp.wait_ge(out_done, START + 16)

            @block.scalar
            def _(act):
                act.wait_ge(c_in, START + 80)
                nc.scalar.activation(ex[:, :, :], cc[:, :, :], ACT.Exp, scale=-1.0).then_inc(e_done, 1)
                if on_scalar:
                    on_scalar(act)

            if on_gpsimd:
                block.gpsimd(on_gpsimd)

            @block.tensor
            def _(pe):
                pe.wait_ge(s_done, START + 3)
                with pe.Fori(0, NCH // 2) as i:
                    for j in range(2):
                        pe.wait_ge(w_in[j], START + (i + 1) * 16)
                        pe.wait_ge(row_ready, START + i * 2)
                        for k in range(KD):
                            mm = nc.tensor.matmul(acc[j][0:2, :], sl[:, k, :], wt[j][:, k, :], start=(k == 0), stop=(k == KD - 1))
                        mm.then_inc(acc_ready[j], 1)
                pe.wait_ge(row_ready, START + NCH)
                for n in range(48):
                    tr = nc.tensor.transpose(colT[:, n, :], row[:, n * 128:(n + 1) * 128], identity[0:2, 0:2])
                tr.then_inc(cols_turned, 1)

            @block.vector
            def _(ve):
                ve.wait_ge(e_done, START + 1)
                nc.vector.tensor_scalar(ex[:, :, :], ex[:, :, :], 1.0, None, ALU.add).then_inc(s_done, 1)
                ve.wait_ge(s_done, START + 1)
                nc.vector.reciprocal(ex[:, :, :], ex[:, :, :]).then_inc(s_done, 1)
                ve.wait_ge(s_done, START + 2)
                nc.vector.tensor_tensor(sl[:, :, :], cc[:, :, :], ex[:, :, :], ALU.mult).then_inc(s_done, 1)
                with ve.Fori(0, NCH // 2) as i:
                    for j in range(2):
                        wait_alone(ve, acc_ready[j], START + i + 1, passed_ve)
                        span = bass.ds((i * 2 + j) * CH, CH)
                        nc.vector.tensor_tensor(row[:, span], acc[j][0:2, :], bias[:, span], ALU.add).then_inc(row_ready, 1)
                ve.wait_ge(cols_turned, START + 1)
                nc.vector.tensor_copy(colS[:, :, :], colT[:, :, :]).then_inc(cols_copied, 1)
                ve.wait_ge(cols_copied, START + 1)
                for half in range(2):
                    sh, sc = half * 24, half * 24 + 8
                    nc.vector.tensor_copy(cols[:, 2 * half + 1, :, :], colS[:, sh:sh + KD, :]).then_inc(chain, 1)
                    g = gain[:, half, :].unsqueeze(2).broadcast_to([128, KD, 2])
                    nc.vector.scalar_tensor_tensor(cols[:, 2 * half, :, :], colS[:, sc:sc + KD, :], 1.0, g, ALU.add, ALU.mult).then_inc(chain, 1)
                ve.wait_ge(chain, START + 4)


def project(nc, name, X, cols_a, cols_b, w, F, CW, out, identity):
    G = 5
    chunks = [(s, min(CW, F - s)) for s in range(0, F, CW)]
    NC = len(chunks)
    BANKS = 5
    with Stage(nc, name) as st:
        sb, ps, sem = st.sb, st.ps, st.sem
        wt = sb("wt", [128, KD, F])
        xn = [sb(f"xn{j}", [128, D]) for j in range(2)]
        hT = [sb(f"hT{j}", [128, KD, 128]) for j in range(2)]
        ot = [sb(f"ot{j}", [128, F]) for j in range(2)]
        rstd = sb("rstd", [128, TILES])
        turned = ps("turned", [128, KD, 128])
        acc = [ps(f"acc{j}", [128, 512]) for j in range(BANKS)]
        w_in, squares, root, rstd_ready = sem("w_in"), sem("squares"), sem("root"), sem("rstd_ready")
        xn_ready, turn_done, h_ready, mm_done = sem("xn_ready"), sem("turn_done"), sem("h_ready"), sem("mm_done")
        tile_mm, taken_v, taken_a, stored, va = sem("tile_mm"), sem("taken_v"), sem("taken_a"), sem("stored"), sem("va")
        passed_sp, passed_ve = sem("passed_sp"), sem("passed_ve")
        odd = [c for c in range(NC) if c % 2]
        even = [c for c in range(NC) if c % 2 == 0]

        def takers(n):
            return n // 2, (n + 1) // 2

        with nc.Block() as block:
            @block.sync
            def _(sp):
                st.open(sp)
                for k in range(KD):
                    sp.dma_start(wt[:, k, :], w[k * 128:(k + 1) * 128, :]).then_inc(w_in, 16)
                with sp.Fori(0, TILES // G) as i:
                    for t in range(G):
                        wait_alone(sp, taken_v, START + (i * G + t + 1) * len(odd), passed_sp)
                        wait_alone(sp, taken_a, START + (i * G + t + 1) * len(even), passed_sp)
                        wait_alone(sp, stored, START + (i * G + t) * 16, passed_sp)
                        sp.dma_start(out[bass.ds((i * G + t) * 128, 128), :], ot[t % 2][:, :]).then_inc(stored, 16)
                        if t == G - 1:
                            wait_alone(sp, stored, START + (i + 1) * G * 16, passed_sp)
                sp.wait_ge(stored, START + TILES * 16)

            @block.scalar
            def _(act):
                with act.Fori(0, TILES) as t:
                    nc.scalar.activation(xn[0][:, :], X[:, bass.ds(t, 1), :], ACT.Square, accum_out=rstd[:, bass.ds(t, 1)]).then_inc(squares, 1)
                    act.wait_ge(squares, START + t + 1)
                act.wait_ge(va, START + 1)
                nc.scalar.activation(rstd[:, :], rstd[:, :], ACT.Sqrt).then_inc(root, 1)
                act.wait_ge(rstd_ready, START + 1)
                with act.Fori(0, TILES // G) as i:
                    def normed(t):
                        act.wait_ge(turn_done, START + i * G + max(t - 1, 0))
                        nc.scalar.activation(xn[t % 2][:, :], X[:, bass.ds(i * G + t, 1), :], ACT.Copy,
                                             scale=rstd[:, bass.ds(i * G + t, 1)]).then_inc(xn_ready, 1)

                    normed(0)
                    for t in range(G):
                        if t + 1 < G:
                            normed(t + 1)
                        for n, c in enumerate(even):
                            act.wait_ge(mm_done, START + (i * G + t) * NC + c + 1)
                            if n == 0:
                                act.wait_ge(stored, START + (i * G + max(t - 1, 0)) * 16)
                            s, m = chunks[c]
                            nc.scalar.activation(ot[t % 2][:, s:s + m], acc[(t * NC + c) % BANKS][:, 0:m], ACT.Copy).then_inc(taken_a, 1)

            @block.tensor
            def _(pe):
                pe.wait_ge(w_in, START + KD * 16)
                with pe.Fori(0, TILES // G) as i:
                    def turn(t):
                        pe.wait_ge(xn_ready, START + i * G + t + 1)
                        pe.wait_ge(h_ready, START + (i * G + t) * KD)
                        for k in range(KD):
                            tr = nc.tensor.transpose(turned[:, k, :], xn[t % 2][:, k * 128:(k + 1) * 128], identity[:, :])
                        tr.then_inc(turn_done, 1)

                    turn(0)
                    for t in range(G):
                        if t + 1 < G:
                            turn(t + 1)
                        pe.wait_ge(h_ready, START + (i * G + t + 1) * KD)
                        for c in range(NC):
                            g = t * NC + c
                            before = g - BANKS + 1
                            if before > 0:
                                bt, bc = divmod(before, NC)
                            else:
                                bt, bc = 0, 0
                            v, a = takers(bc)
                            pe.wait_ge(taken_v, START + (i * G + bt) * len(odd) + v)
                            pe.wait_ge(taken_a, START + (i * G + bt) * len(even) + a)
                            s, m = chunks[c]
                            for k in range(KD):
                                mm = nc.tensor.matmul(acc[g % BANKS][:, 0:m], hT[t % 2][:, k, :], wt[:, k, s:s + m],
                                                      start=(k == 0), stop=(k == KD - 1))
                            mm.then_inc(mm_done, 1)

            @block.vector
            def _(ve):
                ve.wait_ge(squares, START + TILES)
                nc.vector.tensor_scalar(rstd[:, :], rstd[:, :], 1.0 / D, EPS, ALU.mult, ALU.add).then_inc(va, 1)
                ve.wait_ge(root, START + 1)
                nc.vector.reciprocal(rstd[:, :], rstd[:, :]).then_inc(rstd_ready, 1)
                with ve.Fori(0, TILES // G) as i:
                    def modulate(t):
                        wait_alone(ve, turn_done, START + i * G + t + 1, passed_ve)
                        wait_alone(ve, mm_done, START + (i * G + max(t - 1, 0)) * NC, passed_ve)
                        for k in range(KD):
                            if t < CTX_TILES:
                                col = bass.ds(k * 2 + 1 - i, 1)
                            else:
                                col = bass.ds(k * 2, 1)
                            a = cols_a.rearrange("p k c -> p (k c)")[:, col]
                            b = cols_b.rearrange("p k c -> p (k c)")[:, col]
                            nc.vector.tensor_scalar(hT[t % 2][:, k, :], turned[:, k, :], a, b, ALU.mult, ALU.add).then_inc(h_ready, 1)

                    modulate(0)
                    for t in range(G):
                        if t + 1 < G:
                            modulate(t + 1)
                        for n, c in enumerate(odd):
                            wait_alone(ve, mm_done, START + (i * G + t) * NC + c + 1, passed_ve)
                            if n == 0:
                                wait_alone(ve, stored, START + (i * G + max(t - 1, 0)) * 16, passed_ve)
                            s, m = chunks[c]
                            nc.vector.tensor_copy(ot[t % 2][:, s:s + m], acc[(t * NC + c) % BANKS][:, 0:m]).then_inc(taken_v, 1)


def setup(nc, X, identity, x, ctx):
    with Stage(nc, "setup") as st:
        loaded, zeroed, made = st.sem("loaded"), st.sem("zeroed"), st.sem("made")
        with nc.Block() as block:
            @block.sync
            def _(sp):
                st.open(sp)
                sp.dma_start(X[:, 0:CTX_TILES, :], ctx.rearrange("(t p) n -> p t n", p=128)).then_inc(loaded, 16)
                sp.dma_start(X[:, CTX_TILES:TILES, :], x.rearrange("(t p) n -> p t n", p=128)).then_inc(loaded, 16)
                sp.wait_ge(loaded, START + 32)

            @block.gpsimd
            def _(po):
                nc.gpsimd.memset(identity[:, :], 0.0).then_inc(zeroed, 1)
                po.wait_ge(zeroed, START + 1)
                nc.gpsimd.affine_select(out=identity[:, :], in_=identity[:, :], compare_op=ALU.not_equal, fill=1.0,
                                        base=0, pattern=[[-1, 128]], channel_multiplier=1).then_inc(made, 1)
                po.wait_ge(made, START + 1)


def next_context(nc, X, ctx):
    with Stage(nc, "context") as st:
        loaded = st.sem("loaded")
        with nc.Block() as block:
            @block.sync
            def _(sp):
                st.open(sp)
                sp.dma_start(X[:, 0:CTX_TILES, :], ctx.rearrange("(t p) n -> p t n", p=128)).then_inc(loaded, 16)
                sp.wait_ge(loaded, START + 16)


def rotate(eng, out, x, cosines, sines, heads, half, scratch, done, at):
    shape = [128, heads, 2 * half]
    c = cosines.unsqueeze(1).broadcast_to(shape)
    s = sines.rearrange("p (a d) -> p a d", a=2).unsqueeze(1).broadcast_to([128, heads, 2, half])
    swapped = x.rearrange("p h (a d) -> p h a d", a=2)[:, :, ::-1, :]
    t0, t1 = scratch[0][:, 0:heads, 0:2 * half], scratch[1][:, 0:heads, 0:2 * half]
    eng.wait_ge(done, START + at)
    eng.tensor_tensor(t0, x, c, ALU.mult).then_inc(done, 1)
    eng.tensor_tensor(t1.rearrange("p h (a d) -> p h a d", a=2), swapped, s, ALU.mult).then_inc(done, 1)
    eng.wait_ge(done, START + at + 2)
    eng.tensor_tensor(out, t0, t1, ALU.add).then_inc(done, 1)


Q_RANK, KV_RANK, M_HEADS, M_NOPE, M_ROPE, M_V = 256, 128, 6, 64, 32, 64
M_DK = M_NOPE + M_ROPE
S_HEADS, S_KV, S_DK = 6, 2, 64
CONV = 256
IN1 = Q_RANK + KV_RANK + M_ROPE + S_HEADS * S_DK + 2 * S_KV * S_DK + 3 * CONV
O_KR = Q_RANK + KV_RANK
O_SQ = O_KR + M_ROPE
O_SV = O_SQ + (S_HEADS + S_KV) * S_DK
O_B = O_SV + S_KV * S_DK
O_C = O_B + CONV
O_U = O_C + CONV
R_MQ, R_MK = 0, M_HEADS * M_DK
R_SQ = 2 * M_HEADS * M_DK
R_SK = R_SQ + S_HEADS * S_DK
R1 = R_SK + S_KV * S_DK
ZROWS = ROWS + 4


def heads_first(nc, name, P1, table, w_uq, w_ukv, q_gain, kv_gain, RT, V, Z, identity):
    G = 5
    KB = R1 // 128
    QH = M_HEADS * M_DK // 2
    VH = M_HEADS * (M_NOPE + M_V) // 2
    groups = [(g, min(4, KB - g)) for g in range(0, KB, 4)]
    with Stage(nc, name) as st:
        sb, ps, sem = st.sb, st.ps, st.sem
        wq = sb("wq", [128, 2, 2 * QH])
        wkv = sb("wkv", [128, 2 * VH])
        gains = sb("gains", [128, 3])
        p = [sb(f"p{j}", [128, IN1]) for j in range(3)]
        tab = [sb(f"tab{j}", [128, 192]) for j in range(3)]
        junk = sb("junk", [128, Q_RANK])
        ss = [sb(f"ss{j}", [128, 2]) for j in range(2)]
        nrm = [sb(f"nrm{j}", [128, O_KR]) for j in range(2)]
        nrm_kr = [sb(f"nrm_kr{j}", [128, 1, M_ROPE]) for j in range(2)]
        nT = [sb(f"nT{j}", [128, 3, 128]) for j in range(2)]
        row = [sb(f"row{j}", [128, R1]) for j in range(2)]
        vals = [sb(f"vals{j}", [128, M_HEADS, M_V]) for j in range(2)]
        z = [sb(f"z{j}", [128, CONV]) for j in range(2)]
        rT = [sb(f"rT{j}", [128, KB, 128]) for j in range(2)]
        vscratch = [sb(f"vscratch{j}", [128, 8, 64]) for j in range(2)]
        pscratch = [sb(f"pscratch{j}", [128, 8, 64]) for j in range(2)]
        zeros = sb("zeros", [2, CONV])
        tn = ps("tn", [128, 3, 128])
        qa = [ps(f"qa{j}", [128, 512]) for j in range(2)]
        kva = [ps(f"kva{j}", [128, 512]) for j in range(2)]
        tr = [ps(f"tr{j}", [128, 4, 128]) for j in range(3)]
        w_in = sem("w_in")
        p_in = [sem(f"p_in{j}") for j in range(G)]
        squared, meaned, rooted, inverted, normed = sem("squared"), sem("meaned"), sem("rooted"), sem("inverted"), sem("normed")
        n_turned, n_taken, products, q_taken, kv_taken = sem("n_turned"), sem("n_taken"), sem("products"), sem("q_taken"), sem("kv_taken")
        mla_rotated, swa_rotated, kr_rotated, kr_spread, z_made = sem("mla_rotated"), sem("swa_rotated"), sem("kr_rotated"), sem("kr_spread"), sem("z_made")
        turned, taken_v, taken_a = sem("turned"), sem("taken_v"), sem("taken_a")
        stored, zeroed, z_edges = sem("stored"), sem("zeroed"), sem("z_edges")
        passed_sp, passed_ve, passed_po = sem("passed_sp"), sem("passed_ve"), sem("passed_po")
        NG = len(groups)
        NV, NA = NG // 2, (NG + 1) // 2
        rtv = RT.rearrange("(k p) n -> p k n", p=128)
        with nc.Block() as block:
            @block.sync
            def _(sp):
                st.open(sp)
                sp.dma_start(wq[:, :, :], w_uq.rearrange("(k p) n -> p k n", p=128)).then_inc(w_in, 16)
                sp.dma_start(wkv[:, :], w_ukv).then_inc(w_in, 16)
                sp.dma_start(gains[:, 0:2], q_gain.rearrange("(k p) -> p k", p=128), allow_slow_non_contiguous=True).then_inc(w_in, 16)
                sp.dma_start(gains[:, 2:3], kv_gain.rearrange("(k p) -> p k", p=128), allow_slow_non_contiguous=True).then_inc(w_in, 16)
                sp.wait_ge(zeroed, START + 1)
                for r in (0, CTX + 1, CTX + 2, ZROWS - 1):
                    sp.dma_start(Z[r:r + 1, :], zeros[0:1, :]).then_inc(z_edges, 16)
                sp.wait_ge(z_edges, START + 64)
                with sp.Fori(0, TILES // G) as i:
                    for s in range(G + 2):
                        if s < G:
                            n = i * G + s
                            before = i * G + max(s - 2, 0)
                            wait_alone(sp, swa_rotated, START + before * 3, passed_sp)
                            wait_alone(sp, z_made, START + before, passed_sp)
                            wait_alone(sp, mla_rotated, START + before * 3, passed_sp)
                            wait_alone(sp, kr_rotated, START + before * 3, passed_sp)
                            sp.dma_start(p[s % 3][:, :], P1[bass.ds(n * 128, 128), :]).then_inc(p_in[s], 16)
                            sp.dma_start(tab[s % 3][:, :], table[bass.ds(n * 128, 128), :]).then_inc(p_in[s], 16)
                        if s >= 2:
                            t = s - 2
                            n = i * G + t
                            wait_alone(sp, taken_v, START + (n + 1) * NV, passed_sp)
                            wait_alone(sp, taken_a, START + (n + 1) * NA, passed_sp)
                            wait_alone(sp, z_made, START + n + 1, passed_sp)
                            wait_alone(sp, kv_taken, START + (n + 1) * 4, passed_sp)
                            wait_alone(sp, stored, START + n * 48, passed_sp)
                            sp.dma_start(rtv[:, :, bass.ds(n * 128, 128)], rT[t % 2][:, :, :]).then_inc(stored, 16)
                            sp.dma_start(V[bass.ds(n * 128, 128), :], vals[t % 2][:, :, :].rearrange("p h d -> p (h d)")).then_inc(stored, 16)
                            if t < CTX_TILES:
                                first = n * 128 + 1 + i * 2
                            else:
                                first = n * 128 + 3
                            sp.dma_start(Z[bass.ds(first, 128), :], z[t % 2][:, :]).then_inc(stored, 16)
                sp.wait_ge(stored, START + TILES * 48)

            @block.scalar
            def _(act):
                act.wait_ge(w_in, START + 64)
                with act.Fori(0, TILES // G) as i:
                    for s in range(G + 2):
                        if s < G:
                            n = i * G + s
                            act.wait_ge(p_in[s], START + i * 32 + 32)
                            act.wait_ge(normed, START + (i * G + max(s - 1, 0)) * 2)
                            nc.scalar.activation(junk[:, :], p[s % 3][:, 0:Q_RANK], ACT.Square, accum_out=ss[s % 2][:, 0:1]).then_inc(squared, 1)
                            act.wait_ge(squared, START + n * 2 + 1)
                            nc.scalar.activation(junk[:, 0:KV_RANK], p[s % 3][:, Q_RANK:O_KR], ACT.Square, accum_out=ss[s % 2][:, 1:2]).then_inc(squared, 1)
                            act.wait_ge(meaned, START + (n + 1) * 2)
                            nc.scalar.activation(ss[s % 2][:, :], ss[s % 2][:, :], ACT.Sqrt).then_inc(rooted, 1)
                            act.wait_ge(n_turned, START + n + 1)
                            act.wait_ge(products, START + (i * G + max(s - 1, 0)))
                            for k in range(3):
                                nc.scalar.activation(nT[s % 2][:, k, :], tn[:, k, :], ACT.Copy, scale=gains[:, k:k + 1]).then_inc(n_taken, 1)
                        if 1 <= s < G + 1:
                            t = s - 1
                            n = i * G + t
                            act.wait_ge(products, START + n + 1)
                            act.wait_ge(turned, START + (i * G + max(t - 1, 0)) * NG)
                            for h in range(2):
                                nc.scalar.activation(row[t % 2][:, h * QH:(h + 1) * QH], qa[h][:, 0:QH], ACT.Copy).then_inc(q_taken, 1)
                        if s >= 2:
                            t = s - 2
                            n = i * G + t
                            act.wait_ge(stored, START + (i * G + max(t - 1, 0)) * 48)
                            for g, (b, m) in enumerate(groups):
                                if g % 2 == 0:
                                    act.wait_ge(turned, START + n * NG + g + 1)
                                    nc.scalar.activation(rT[t % 2][:, b:b + m, :], tr[(g + t) % 3][:, 0:m, :], ACT.Copy).then_inc(taken_a, 1)

            @block.tensor
            def _(pe):
                pe.wait_ge(w_in, START + 64)
                with pe.Fori(0, TILES // G) as i:
                    for s in range(G + 2):
                        if s < G:
                            n = i * G + s
                            pe.wait_ge(normed, START + (n + 1) * 2)
                            pe.wait_ge(n_taken, START + n * 3)
                            for k in range(3):
                                tp = nc.tensor.transpose(tn[:, k, :], nrm[s % 2][:, k * 128:(k + 1) * 128], identity[:, :])
                            tp.then_inc(n_turned, 1)
                        if 1 <= s < G + 1:
                            n = i * G + s - 1
                            t = s - 1
                            pe.wait_ge(n_taken, START + (n + 1) * 3)
                            pe.wait_ge(q_taken, START + n * 2)
                            pe.wait_ge(kv_taken, START + n * 4)
                            for h in range(2):
                                for k in range(2):
                                    nc.tensor.matmul(qa[h][:, 0:QH], nT[t % 2][:, k, :], wq[:, k, h * QH:(h + 1) * QH], start=(k == 0), stop=(k == 1))
                            for h in range(2):
                                mm = nc.tensor.matmul(kva[h][:, 0:VH], nT[t % 2][:, 2, :], wkv[:, h * VH:(h + 1) * VH], start=True, stop=True)
                            mm.then_inc(products, 1)
                        if s >= 2:
                            t = s - 2
                            n = i * G + t
                            pe.wait_ge(mla_rotated, START + (n + 1) * 3)
                            pe.wait_ge(kv_taken, START + (n + 1) * 4)
                            pe.wait_ge(swa_rotated, START + (n + 1) * 3)
                            pe.wait_ge(kr_spread, START + n + 1)
                            for g, (b, m) in enumerate(groups):
                                bt, bg = divmod(max(t * NG + g - 2, 0), NG)
                                pe.wait_ge(taken_v, START + (i * G + bt) * NV + bg // 2)
                                pe.wait_ge(taken_a, START + (i * G + bt) * NA + (bg + 1) // 2)
                                for k in range(m):
                                    tp = nc.tensor.transpose(tr[(g + t) % 3][:, k, :], row[t % 2][:, (b + k) * 128:(b + k + 1) * 128], identity[:, :])
                                tp.then_inc(turned, 1)

            @block.vector
            def _(ve):
                with ve.Fori(0, TILES // G) as i:
                    for s in range(G + 2):
                        if s < G:
                            n = i * G + s
                            wait_alone(ve, squared, START + (n + 1) * 2, passed_ve)
                            nc.vector.tensor_scalar(ss[s % 2][:, 0:1], ss[s % 2][:, 0:1], 1.0 / Q_RANK, EPS, ALU.mult, ALU.add).then_inc(meaned, 1)
                            nc.vector.tensor_scalar(ss[s % 2][:, 1:2], ss[s % 2][:, 1:2], 1.0 / KV_RANK, EPS, ALU.mult, ALU.add).then_inc(meaned, 1)
                            wait_alone(ve, rooted, START + n + 1, passed_ve)
                            nc.vector.reciprocal(ss[s % 2][:, :], ss[s % 2][:, :]).then_inc(inverted, 1)
                            wait_alone(ve, inverted, START + n + 1, passed_ve)
                            wait_alone(ve, n_turned, START + (i * G + max(s - 1, 0)), passed_ve)
                            nc.vector.tensor_scalar(nrm[s % 2][:, 0:Q_RANK], p[s % 3][:, 0:Q_RANK], ss[s % 2][:, 0:1], None, ALU.mult).then_inc(normed, 1)
                            nc.vector.tensor_scalar(nrm[s % 2][:, Q_RANK:O_KR], p[s % 3][:, Q_RANK:O_KR], ss[s % 2][:, 1:2], None, ALU.mult).then_inc(normed, 1)
                        if 1 <= s < G + 1:
                            t = s - 1
                            n = i * G + t
                            rw = row[t % 2]
                            wait_alone(ve, turned, START + (i * G + max(t - 1, 0)) * NG, passed_ve)
                            sq = p[t % 3][:, O_SQ:O_SV].rearrange("p (h d) -> p h d", d=S_DK)
                            rotate(nc.vector, rw[:, R_SQ:R1].rearrange("p (h d) -> p h d", d=S_DK), sq, tab[t % 3][:, 64:128], tab[t % 3][:, 128:192],
                                   S_HEADS + S_KV, S_DK // 2, vscratch, swa_rotated, n * 3)
                            wait_alone(ve, stored, START + (i * G + max(t - 1, 0)) * 48, passed_ve)
                            wait_alone(ve, products, START + n + 1, passed_ve)
                            mk = rw[:, R_MK:R_SQ].rearrange("p (h d) -> p h d", d=M_DK)
                            hh = M_HEADS // 2
                            for h in range(2):
                                kv = kva[h][:, 0:VH].rearrange("p (h d) -> p h d", d=M_NOPE + M_V)
                                nc.vector.tensor_copy(mk[:, h * hh:(h + 1) * hh, 0:M_NOPE], kv[:, :, 0:M_NOPE]).then_inc(kv_taken, 1)
                                nc.vector.tensor_copy(vals[t % 2][:, h * hh:(h + 1) * hh, :], kv[:, :, M_NOPE:]).then_inc(kv_taken, 1)
                            wait_alone(ve, kr_rotated, START + (n + 1) * 3, passed_ve)
                            kr = nrm_kr[t % 2][:, :, :].broadcast_to([128, M_HEADS, M_ROPE])
                            nc.vector.tensor_copy(mk[:, :, M_NOPE:], kr).then_inc(kr_spread, 1)
                        if s >= 2:
                            t = s - 2
                            n = i * G + t
                            wait_alone(ve, stored, START + (i * G + max(t - 1, 0)) * 48, passed_ve)
                            for g, (b, m) in enumerate(groups):
                                if g % 2:
                                    wait_alone(ve, turned, START + n * NG + g + 1, passed_ve)
                                    nc.vector.tensor_copy(rT[t % 2][:, b:b + m, :], tr[(g + t) % 3][:, 0:m, :]).then_inc(taken_v, 1)

            @block.gpsimd
            def _(po):
                nc.gpsimd.memset(zeros[:, :], 0.0).then_inc(zeroed, 1)
                with po.Fori(0, TILES // G) as i:
                    for t in range(G):
                        n = i * G + t
                        wait_alone(po, p_in[t], START + i * 32 + 32, passed_po)
                        wait_alone(po, kr_spread, START + (i * G + max(t - 1, 0)), passed_po)
                        kr = p[t % 3][:, O_KR:O_SQ].unsqueeze(1)
                        rotate(nc.gpsimd, nrm_kr[t % 2][:, :, :], kr, tab[t % 3][:, 0:32], tab[t % 3][:, 32:64], 1, M_ROPE // 2, pscratch, kr_rotated, n * 3)
                        wait_alone(po, stored, START + (i * G + max(t - 1, 0)) * 48, passed_po)
                        nc.gpsimd.tensor_tensor(z[t % 2][:, :], p[t % 3][:, O_C:O_U], p[t % 3][:, O_U:IN1], ALU.mult).then_inc(z_made, 1)
                        wait_alone(po, kr_rotated, START + (n + 1) * 3, passed_po)
                        wait_alone(po, q_taken, START + (n + 1) * 2, passed_po)
                        mq = row[t % 2][:, R_MQ:R_MK].rearrange("p (h d) -> p h d", d=M_DK)[:, :, M_NOPE:]
                        rotate(nc.gpsimd, mq, mq, tab[t % 3][:, 0:32], tab[t % 3][:, 32:64], M_HEADS, M_ROPE // 2, pscratch, mla_rotated, n * 3)
                        wait_alone(po, mla_rotated, START + (n + 1) * 3, passed_po)


def attend(nc, name, turns, slots, DK, DV, scale, q_of, k_of, v_of, k_shared, v_shared, units, out_of, identity,
           masks=None, sink=None, bias_of=None):
    lifted_scores = masks is not None or bias_of is not None
    U = slots * len(units)
    work = []
    for a in range(slots):
        for q, (row, ranges, mask) in enumerate(units):
            work.append((a, q, row, ranges, mask))
    blocks = [[r // 128 + j for r, m in w[3] for j in range(m // 128)] for w in work]
    ngroups = [(len(b) + 3) // 4 for b in blocks]
    first_group = [sum(ngroups[:u]) for u in range(U + 1)]
    TG = first_group[U]
    first_v = [first_group[u] - u for u in range(U + 1)]
    TV = first_v[U]
    lifts = [1 + (w[4] is not None) for w in work]
    first_lift = [sum(lifts[:u]) for u in range(U + 1)] if lifted_scores else None
    NK = max(sum(m for _, m in w[3]) for w in work)
    FIN = 3 if sink is not None else 2
    with Stage(nc, name) as st:
        sb, ps, sem = st.sb, st.ps, st.sem
        qT = [sb(f"qT{a}", [DK, ROWS]) for a in range(slots)]
        kT = [sb(f"kT{a}", [DK, ROWS]) for a in range(1 if k_shared else slots)]
        v = [sb(f"v{a}", [128, TILES, DV]) for a in range(1 if v_shared else slots)]
        prob = [sb(f"prob{j}", [128, NK]) for j in range(2)]
        probT = [sb(f"probT{j}", [128, 4, 128]) for j in range(3)]
        o = [sb(f"o{j}", [128, DV]) for j in range(2)]
        top = [sb(f"top{j}", [128, 1]) for j in range(2)]
        shift = [sb(f"shift{j}", [128, 1]) for j in range(2)]
        total = [sb(f"total{j}", [128, 1]) for j in range(2)]
        inv = [sb(f"inv{j}", [128, 1]) for j in range(2)]
        if lifted_scores:
            raised = [sb(f"raised{j}", [128, NK]) for j in range(2)]
        if masks is not None:
            mask_sb = sb("mask", [128, masks.shape[1]])
        if bias_of is not None:
            bias_sb = [sb(f"bias{a}", [128, bias_of(0, 0).shape[1]]) for a in range(slots)]
        if sink is not None:
            H = sink.shape[0]
            sinks = sb("sinks", [128, H])
            less_sinks = sb("less_sinks", [128, H])
            sunk = [sb(f"sunk{j}", [128, 1]) for j in range(2)]
            whole = [sb(f"whole{j}", [128, 1]) for j in range(2)]
        scores = ps("scores", [128, 1536])
        turnedP = [ps(f"turned{j}", [128, 4, 128]) for j in range(3)]
        mixed = [ps(f"mixed{j}", [128, 512]) for j in range(2)]
        head_in = [sem(f"head_in{a}") for a in range(slots)]
        const_in, negated = sem("const_in"), sem("negated")
        scored, maxed, lifted, topped = sem("scored"), sem("maxed"), sem("lifted"), sem("topped")
        raised_p, sink_raised = sem("exps"), sem("sink_exps")
        turned, taken_a, taken_v, mixed_g = sem("turned"), sem("taken_a"), sem("taken_v"), sem("mixed_g")
        summed, finished, stored = sem("summed"), sem("finished"), sem("stored")
        passed_sp, passed_ve, passed_act = sem("passed_sp"), sem("passed_ve"), sem("passed_act")
        loads = [(1 if (k_shared and a) else 0) + (1 if (v_shared and a) else 0) for a in range(slots)]
        n_in = [(3 - loads[a]) * 16 + (16 if bias_of is not None else 0) for a in range(slots)]
        with nc.Block() as block:
            @block.sync
            def _(sp):
                st.open(sp)
                if masks is not None:
                    sp.dma_start(mask_sb[:, :], masks).then_inc(const_in, 16)
                if sink is not None:
                    sp.dma_start(sinks[:, :], sink.partition_broadcast(128)).then_inc(const_in, 16)
                def load(it, a, shared):
                    if not shared:
                        sp.dma_start(qT[a][:, :], q_of(it, a)).then_inc(head_in[a], 16)
                        if bias_of is not None:
                            sp.dma_start(bias_sb[a][:, :], bias_of(it, a)).then_inc(head_in[a], 16)
                    if k_shared == shared:
                        sp.dma_start(kT[a][:, :], k_of(it, a)).then_inc(head_in[a], 16)
                    if v_shared == shared:
                        sp.dma_start(v[a][:, :, :], v_of(it, a)).then_inc(head_in[a], 16)

                def store(it, u):
                    a, q, row, _, _ = work[u]
                    wait_alone(sp, finished, START + (it * U + u + 1) * FIN, passed_sp)
                    wait_alone(sp, stored, START + (it * U + u) * 16, passed_sp)
                    sp.dma_start(out_of(it, a, row), o[u % 2][:, :]).then_inc(stored, 16)

                load(0, 0, True)
                for a in range(slots):
                    load(0, a, False)
                with sp.Fori(0, turns - 1) as it:
                    for u in range(U):
                        store(it, u)
                        if u + 1 == U or work[u + 1][0] != work[u][0]:
                            wait_alone(sp, mixed_g, START + it * TG + first_group[u + 1], passed_sp)
                            if u + 1 == U:
                                load(it + 1, 0, True)
                            load(it + 1, work[u][0], False)
                for u in range(U):
                    store(turns - 1, u)
                sp.wait_ge(stored, START + turns * U * 16)

            @block.tensor
            def _(pe):
                with pe.Fori(0, turns) as it:
                    def score(u):
                        a, q, row, ranges, _ = work[u]
                        if q == 0:
                            pe.wait_ge(head_in[a], START + it * n_in[a] + n_in[a])
                        if lifted_scores:
                            pe.wait_ge(lifted, START + it * first_lift[U] + first_lift[u])
                            pe.wait_ge(raised_p, START + it * U + max(u - 1, 0))
                        else:
                            pe.wait_ge(raised_p, START + it * U + u)
                        at = 0
                        for r, m in ranges:
                            while m:
                                n = min(m, 512 - at % 512)
                                mm = nc.tensor.matmul(scores[:, at:at + n], qT[a][:, row:row + 128], kT[0 if k_shared else a][:, r:r + n],
                                                      start=True, stop=True)
                                at, r, m = at + n, r + n, m - n
                        mm.then_inc(scored, 1)

                    def turn(u, g):
                        G = first_group[u] + g
                        b = max(G - 2, 0)
                        bu = max(x for x in range(U) if first_group[x] <= b)
                        within = b - first_group[bu]
                        pe.wait_ge(taken_a, START + it * U + bu + (within > 0))
                        pe.wait_ge(taken_v, START + it * TV + first_v[bu] + max(within - 1, 0))
                        for j in range(4 * g, min(4 * g + 4, len(blocks[u]))):
                            tp = nc.tensor.transpose(turnedP[G % 3][:, j % 4, :], prob[u % 2][:, j * 128:(j + 1) * 128], identity[:, :])
                        tp.then_inc(turned, 1)

                    def mix(u, g):
                        a = work[u][0]
                        G = first_group[u] + g
                        if g == 0:
                            pe.wait_ge(taken_a, START + it * U + u + 1)
                            pe.wait_ge(finished, START + (it * U + max(u - 1, 0)) * FIN)
                        else:
                            pe.wait_ge(taken_v, START + it * TV + first_v[u] + g)
                        n = len(blocks[u])
                        for j in range(4 * g, min(4 * g + 4, n)):
                            mm = nc.tensor.matmul(mixed[u % 2][:, 0:DV], probT[G % 3][:, j % 4, :], v[0 if v_shared else a][:, blocks[u][j], :],
                                                  start=(j == 0), stop=(j == n - 1))
                        mm.then_inc(mixed_g, 1)

                    score(0)
                    for u in range(U):
                        if u + 1 < U:
                            score(u + 1)
                        pe.wait_ge(raised_p, START + it * U + u + 1)
                        for g in range(ngroups[u]):
                            turn(u, g)
                            if g:
                                mix(u, g - 1)
                        mix(u, ngroups[u] - 1)

            @block.scalar
            def _(act):
                if sink is not None:
                    act.wait_ge(const_in, START + 16 * (1 + (masks is not None)))
                    nc.scalar.activation(less_sinks[:, :], sinks[:, :], ACT.Copy, scale=-1.0).then_inc(negated, 1)
                with act.Fori(0, turns) as it:
                    def exps(u):
                        nk = len(blocks[u]) * 128
                        act.wait_ge(maxed, START + it * U + u + 1)
                        act.wait_ge(turned, START + it * TG + first_group[max(u - 1, 0)])
                        act.wait_ge(finished, START + (it * U + max(u - 1, 0)) * FIN)
                        if sink is not None:
                            act.sem_inc(passed_act, 1)
                            h = it * slots + work[u][0]
                            nc.scalar.activation(sunk[u % 2][:, :], sinks[:, bass.ds(h, 1)], ACT.Exp, bias=shift[u % 2][:, :]).then_inc(sink_raised, 1)
                        src = raised[u % 2][:, 0:nk] if lifted_scores else scores[:, 0:nk]
                        nc.scalar.activation(prob[u % 2][:, 0:nk], src, ACT.Exp, bias=shift[u % 2][:, :],
                                             scale=1.0 if lifted_scores else scale, accum_out=total[u % 2][:, :]).then_inc(raised_p, 1)

                    exps(0)
                    for u in range(U):
                        G = first_group[u]
                        m = min(4, len(blocks[u]))
                        act.wait_ge(turned, START + it * TG + G + 1)
                        act.wait_ge(mixed_g, START + it * TG + max(G - 2, 0))
                        nc.scalar.activation(probT[G % 3][:, 0:m, :], turnedP[G % 3][:, 0:m, :], ACT.Copy).then_inc(taken_a, 1)
                        if u + 1 < U:
                            exps(u + 1)

            @block.vector
            def _(ve):
                if masks is not None or sink is not None:
                    ve.wait_ge(const_in, START + 16 * ((masks is not None) + (sink is not None)))
                if sink is not None:
                    ve.wait_ge(negated, START + 1)
                with ve.Fori(0, turns) as it:
                    def maximum(u):
                        a, q, row, ranges, mask = work[u]
                        nk = len(blocks[u]) * 128
                        if bias_of is not None and q == 0:
                            wait_alone(ve, head_in[a], START + it * n_in[a] + n_in[a], passed_ve)
                        wait_alone(ve, scored, START + it * U + u + 1, passed_ve)
                        wait_alone(ve, raised_p, START + it * U + max(u - 1, 0), passed_ve)
                        src = scores[:, 0:nk]
                        if lifted_scores:
                            src = raised[u % 2][:, 0:nk]
                            split = ranges[0][1] if mask is not None else nk
                            ins = nc.vector.tensor_scalar(raised[u % 2][:, 0:split], scores[:, 0:split], scale, None, ALU.mult)
                            ins.then_inc(lifted, 1)
                            if mask is not None:
                                m0, mw = mask
                                table = mask_sb if masks is not None else bias_sb[a]
                                nc.vector.scalar_tensor_tensor(raised[u % 2][:, split:nk], scores[:, split:nk], scale, table[:, m0:m0 + mw],
                                                               ALU.mult, ALU.add).then_inc(lifted, 1)
                            wait_alone(ve, lifted, START + it * first_lift[U] + first_lift[u + 1], passed_ve)
                        wait_alone(ve, maxed, START + it * U + max(u - 1, 0), passed_ve)
                        if sink is not None:
                            wait_alone(ve, sink_raised, START + it * U + max(u - 1, 0), passed_ve)
                        nc.vector.tensor_reduce(top[u % 2][:, :], src, AX.X, ALU.max, negate=True).then_inc(topped, 1)
                        wait_alone(ve, topped, START + it * U + u + 1, passed_ve)
                        if sink is not None:
                            nc.vector.tensor_tensor(shift[u % 2][:, :], top[u % 2][:, :], less_sinks[:, bass.ds(it * slots + a, 1)], ALU.min).then_inc(maxed, 1)
                        else:
                            nc.vector.tensor_scalar(shift[u % 2][:, :], top[u % 2][:, :], 1.0 if lifted_scores else scale, None, ALU.mult).then_inc(maxed, 1)

                    maximum(0)
                    for u in range(U):
                        if u + 1 < U:
                            maximum(u + 1)
                        for g in range(1, ngroups[u]):
                            G = first_group[u] + g
                            m = min(4, len(blocks[u]) - 4 * g)
                            wait_alone(ve, turned, START + it * TG + G + 1, passed_ve)
                            wait_alone(ve, mixed_g, START + it * TG + max(G - 2, 0), passed_ve)
                            nc.vector.tensor_copy(probT[G % 3][:, 0:m, :], turnedP[G % 3][:, 0:m, :]).then_inc(taken_v, 1)
                        base = (it * U + u) * FIN
                        wait_alone(ve, raised_p, START + it * U + u + 1, passed_ve)
                        wait_alone(ve, finished, START + base, passed_ve)
                        s = total[u % 2]
                        k = 0
                        if sink is not None:
                            wait_alone(ve, sink_raised, START + it * U + u + 1, passed_ve)
                            nc.vector.tensor_tensor(whole[u % 2][:, :], total[u % 2][:, :], sunk[u % 2][:, :], ALU.add).then_inc(finished, 1)
                            k, s = 1, whole[u % 2]
                            wait_alone(ve, finished, START + base + 1, passed_ve)
                        nc.vector.reciprocal(inv[u % 2][:, :], s[:, :]).then_inc(finished, 1)
                        wait_alone(ve, finished, START + base + k + 1, passed_ve)
                        wait_alone(ve, mixed_g, START + it * TG + first_group[u + 1], passed_ve)
                        wait_alone(ve, stored, START + (it * U + max(u - 1, 0)) * 16, passed_ve)
                        nc.vector.tensor_scalar(o[u % 2][:, :], mixed[u % 2][:, 0:DV], inv[u % 2][:, 0:1], None, ALU.mult).then_inc(finished, 1)


def mla_attention(nc, name, RT, V, mix, identity, with_context):
    units = [(CTX + 128 * t, [(0, ROWS)], None) for t in range(LAT_TILES)]
    if with_context:
        units = [(128 * t, [(0, CTX)], None) for t in range(CTX_TILES)] + units
    slots = 2
    vv = V.rearrange("(t p) n -> p t n", p=128)
    attend(nc, name, M_HEADS // slots, slots, M_DK, M_V, M_DK ** -0.5,
           lambda it, a: RT[bass.ds((it * slots + a) * M_DK + R_MQ, M_DK), :],
           lambda it, a: RT[bass.ds((it * slots + a) * M_DK + R_MK, M_DK), :],
           lambda it, a: vv[:, :, bass.ds((it * slots + a) * M_V, M_V)],
           False, False, units, lambda it, a, row: mix[row:row + 128, bass.ds((it * slots + a) * M_V, M_V)], identity)


def swa_attention(nc, name, RT, P1, mix, masks, sink, identity, with_context):
    units = []
    if with_context:
        units = [(128 * t, [(0, CTX)], None) for t in range(CTX_TILES)]
    for t in range(LAT_TILES):
        lo, hi = max(t - 1, 0), min(t + 2, LAT_TILES)
        units.append((CTX + 128 * t, [(0, CTX), (CTX + 128 * lo, 128 * (hi - lo))], (128 * (lo - t + 1), 128 * (hi - lo))))
    slots = S_HEADS // S_KV
    vv = P1.rearrange("(t p) n -> p t n", p=128)
    base = M_HEADS * M_V
    attend(nc, name, S_KV, slots, S_DK, S_DK, S_DK ** -0.5,
           lambda it, a: RT[bass.ds((it * slots + a) * S_DK + R_SQ, S_DK), :],
           lambda it, a: RT[bass.ds(it * S_DK + R_SK, S_DK), :],
           lambda it, a: vv[:, :, bass.ds(it * S_DK + O_SV, S_DK)],
           True, True, units, lambda it, a, row: mix[row:row + 128, bass.ds((it * slots + a) * S_DK + base, S_DK)], identity,
           masks=masks, sink=sink)


def mix_out(nc, name, first, count, mix, w_o, gate, X, identity, conv=None):
    B = 2
    width = D - (CONV if conv else 0)
    per_tile = 80 if conv else 16
    with Stage(nc, name) as st:
        sb, ps, sem = st.sb, st.ps, st.sem
        wt = sb("wt", [128, KD, D])
        gt = sb("gt", [128, D])
        m = [sb(f"m{j}", [128, D]) for j in range(B)]
        mT = [sb(f"mT{j}", [128, KD, 128]) for j in range(B)]
        gated = [sb(f"gated{j}", [128, D]) for j in range(B)]
        turnedP = [ps(f"turned{j}", [128, KD, 128]) for j in range(B)]
        acc = [ps(f"acc{j}", [128, D]) for j in range(B)]
        if conv:
            P1, Z, conv_w, shift = conv
            taps = sb("taps", [128, 3, CONV])
            z = [sb(f"z{j}", [128, 3, CONV]) for j in range(B)]
            bg = [sb(f"bg{j}", [128, CONV]) for j in range(B)]
            part = [sb(f"part{j}", [128, CONV]) for j in range(B)]
        w_in, steps = sem("w_in"), sem("steps")
        m_in, conv_made, turned, taken_a, taken_v, projected, gated_s, added = (
            [sem(f"{n}{j}") for j in range(B)] for n in ("m_in", "conv_made", "turned", "taken_a", "taken_v", "projected", "gated_s", "added"))
        passed_sp, passed_ve, passed_po = sem("passed_sp"), sem("passed_ve"), sem("passed_po")
        NCONST = 2 + (1 if conv else 0)
        with nc.Block() as block:
            @block.sync
            def _(sp):
                st.open(sp)
                sp.dma_start(gt[:, :], gate.partition_broadcast(128)).then_inc(w_in, 16)
                if conv:
                    sp.dma_start(taps[:, :, :], conv_w.rearrange("k n -> (k n)").partition_broadcast(128)).then_inc(w_in, 16)
                sp.dma_start(wt[:, :, :], w_o.rearrange("(k p) n -> p k n", p=128)).then_inc(w_in, 16)
                with sp.Fori(0, count // B) as i:
                    for j in range(B):
                        wait_alone(sp, turned[j], START + i, passed_sp)
                        row = (first + i * B + j) * 128
                        sp.dma_start(m[j][:, 0:width], mix[bass.ds(row, 128), 0:width]).then_inc(m_in[j], 16)
                        if conv:
                            wait_alone(sp, conv_made[j], START + i * 6, passed_sp)
                            sp.dma_start(bg[j][:, :], P1[bass.ds(row, 128), O_B:O_C]).then_inc(m_in[j], 16)
                            for k in range(3):
                                sp.dma_start(z[j][:, k, :], Z[bass.ds(row + shift + k - 1, 128), :]).then_inc(m_in[j], 16)

            @block.gpsimd
            def _(po):
                if conv:
                    po.wait_ge(w_in, START + 16 * NCONST)
                    with po.Fori(0, count // B) as i:
                        for j in range(B):
                            wait_alone(po, m_in[j], START + (i + 1) * per_tile, passed_po)
                            t = nc.gpsimd
                            c = conv_made[j]
                            t.tensor_tensor(z[j][:, 0, :], z[j][:, 0, :], taps[:, 0, :], ALU.mult).then_inc(c, 1)
                            t.tensor_tensor(z[j][:, 1, :], z[j][:, 1, :], taps[:, 1, :], ALU.mult).then_inc(c, 1)
                            t.tensor_tensor(z[j][:, 2, :], z[j][:, 2, :], taps[:, 2, :], ALU.mult).then_inc(c, 1)
                            wait_alone(po, c, START + i * 6 + 3, passed_po)
                            t.tensor_tensor(part[j][:, :], z[j][:, 0, :], z[j][:, 1, :], ALU.add).then_inc(c, 1)
                            wait_alone(po, c, START + i * 6 + 4, passed_po)
                            t.tensor_tensor(part[j][:, :], part[j][:, :], z[j][:, 2, :], ALU.add).then_inc(c, 1)
                            wait_alone(po, c, START + i * 6 + 5, passed_po)
                            t.tensor_tensor(m[j][:, width:D], part[j][:, :], bg[j][:, :], ALU.mult).then_inc(c, 1)
                            wait_alone(po, c, START + i * 6 + 6, passed_po)

            @block.scalar
            def _(act):
                with act.Fori(0, count // B) as i:
                    for j in range(B):
                        act.wait_ge(turned[j], START + i + 1)
                        act.wait_ge(projected[j], START + i)
                        nc.scalar.activation(mT[j][:, 0:4, :], turnedP[j][:, 0:4, :], ACT.Copy).then_inc(taken_a[j], 1)

            @block.tensor
            def _(pe):
                with pe.Fori(0, count // B) as i:
                    def turn(j):
                        pe.wait_ge(m_in[j], START + (i + 1) * per_tile)
                        if conv:
                            pe.wait_ge(conv_made[j], START + (i + 1) * 6)
                        pe.wait_ge(taken_a[j], START + i)
                        pe.wait_ge(taken_v[j], START + i)
                        for k in range(KD):
                            tp = nc.tensor.transpose(turnedP[j][:, k, :], m[j][:, k * 128:(k + 1) * 128], identity[:, :])
                        tp.then_inc(turned[j], 1)

                    def project_tile(j):
                        pe.wait_ge(taken_a[j], START + i + 1)
                        pe.wait_ge(taken_v[j], START + i + 1)
                        pe.wait_ge(gated_s[j], START + i)
                        for c in range(2):
                            for k in range(KD):
                                mm = nc.tensor.matmul(acc[j][:, c * 512:(c + 1) * 512], mT[j][:, k, :], wt[:, k, c * 512:(c + 1) * 512],
                                                      start=(k == 0), stop=(k == KD - 1))
                        mm.then_inc(projected[j], 1)

                    turn(0)
                    turn(1)
                    pe.wait_ge(w_in, START + 16 * NCONST)
                    project_tile(0)
                    project_tile(1)

            @block.vector
            def _(ve):
                ve.wait_ge(w_in, START + 16 * NCONST)
                with ve.Fori(0, count // B) as i:
                    for j in range(B):
                        wait_alone(ve, turned[j], START + i + 1, passed_ve)
                        wait_alone(ve, projected[j], START + i, passed_ve)
                        nc.vector.tensor_copy(mT[j][:, 4:8, :], turnedP[j][:, 4:8, :]).then_inc(taken_v[j], 1)
                    for j in range(B):
                        wait_alone(ve, projected[j], START + i + 1, passed_ve)
                        wait_alone(ve, added[j], START + i, passed_ve)
                        nc.vector.tensor_tensor(gated[j][:, :], acc[j][:, :], gt[:, :], ALU.mult).then_inc(gated_s[j], 1)
                        wait_alone(ve, gated_s[j], START + i + 1, passed_ve)
                        xt = X[:, bass.ds(first + i * B + j, 1), :].rearrange("p a n -> p (a n)")
                        nc.vector.tensor_tensor(xt, xt, gated[j][:, :], ALU.add).then_inc(added[j], 1)
                ve.wait_ge(added[0], START + count // B)
                ve.wait_ge(added[1], START + count // B)


def route_choice(nc, name, first, count, X, cols_a, cols_b, col, router_w, XN, cap, choice_idx, choice_aff, identity):
    E = 16
    rows = count * 128
    B = 2
    with Stage(nc, name) as st:
        sb, ps, sem = st.sb, st.ps, st.sem
        rw = sb("rw", [128, KD, E])
        ssum = sb("ssum", [128, count])
        junk = sb("junk", [128, D])
        xn = [sb(f"xn{j}", [128, D]) for j in range(B)]
        hT = [sb(f"hT{j}", [128, KD, 128]) for j in range(B)]
        aff = [sb(f"aff{j}", [128, E]) for j in range(B)]
        top = [sb(f"top{j}", [128, 1]) for j in range(B)]
        den = [sb(f"den{j}", [128, 1]) for j in range(B)]
        affT = sb("affT", [E, rows])
        chosen = sb("chosen", [E, cap])
        chosen_at = sb("chosen_at", [E, cap], u32)
        chosen_f = sb("chosen_f", [E, cap])
        turnedP = [ps(f"turned{j}", [128, KD, 128]) for j in range(B)]
        logits = [ps(f"logits{j}", [128, 512]) for j in range(B)]
        small = [ps(f"small{j}", [128, 512]) for j in range(B)]
        w_in, squares, mean, root, inv = sem("w_in"), sem("squares"), sem("mean"), sem("root"), sem("inv")
        normed, stored, turned, h_ready, scored, maxed, raised, inverted, weighed, aff_turned, aff_taken = (
            [sem(f"{n}{j}") for j in range(B)] for n in ("normed", "stored", "turned", "h_ready", "scored", "maxed", "raised", "inverted",
                                                         "weighed", "aff_turned", "aff_taken"))
        found, numbered, final_turned, final_taken = sem("found"), sem("numbered"), sem("final_turned"), sem("final_taken")
        passed_sp, passed_ve, passed_act = sem("passed_sp"), sem("passed_ve"), sem("passed_act")
        with nc.Block() as block:
            @block.sync
            def _(sp):
                st.open(sp)
                sp.dma_start(rw[:, :, :], router_w.rearrange("(k p) e -> p k e", p=128)).then_inc(w_in, 16)
                with sp.Fori(0, count // B) as i:
                    for j in range(B):
                        wait_alone(sp, normed[j], START + i + 1, passed_sp)
                        sp.dma_start(XN[bass.ds((first + i * B + j) * 128, 128), :], xn[j][:, :]).then_inc(stored[j], 16)
                for j in range(B):
                    sp.wait_ge(stored[j], START + count // B * 16)

            @block.scalar
            def _(act):
                for t in range(count):
                    if t:
                        act.wait_ge(squares, START + t)
                    nc.scalar.activation(junk[:, :], X[:, first + t, :], ACT.Square, accum_out=ssum[:, t:t + 1]).then_inc(squares, 1)
                act.wait_ge(mean, START + 1)
                nc.scalar.activation(ssum[:, :], ssum[:, :], ACT.Sqrt).then_inc(root, 1)
                act.wait_ge(inv, START + 1)
                with act.Fori(0, count // B) as i:
                    for j in range(B):
                        act.wait_ge(stored[j], START + i * 16)
                        act.wait_ge(turned[j], START + i)
                        act.sem_inc(passed_act, 1)
                        nc.scalar.activation(xn[j][:, :], X[:, bass.ds(first + i * B + j, 1), :], ACT.Copy,
                                             scale=ssum[:, bass.ds(i * B + j, 1)]).then_inc(normed[j], 1)
                    for j in range(B):
                        act.wait_ge(maxed[j], START + i + 1)
                        nc.scalar.activation(aff[j][:, :], logits[j][:, 0:E], ACT.Exp, bias=top[j][:, :], accum_out=den[j][:, :]).then_inc(raised[j], 1)

            @block.tensor
            def _(pe):
                pe.wait_ge(w_in, START + 16)
                with pe.Fori(0, count // B) as i:
                    for j in range(B):
                        pe.wait_ge(normed[j], START + i + 1)
                        pe.wait_ge(h_ready[j], START + i * KD)
                        for k in range(KD):
                            tp = nc.tensor.transpose(turnedP[j][:, k, :], xn[j][:, k * 128:(k + 1) * 128], identity[:, :])
                        tp.then_inc(turned[j], 1)
                    for j in range(B):
                        pe.wait_ge(h_ready[j], START + (i + 1) * KD)
                        pe.wait_ge(raised[j], START + i)
                        for k in range(KD):
                            mm = nc.tensor.matmul(logits[j][:, 0:E], hT[j][:, k, :], rw[:, k, :], start=(k == 0), stop=(k == KD - 1))
                        mm.then_inc(scored[j], 1)
                    for j in range(B):
                        pe.wait_ge(weighed[j], START + i + 1)
                        pe.wait_ge(aff_taken[j], START + i)
                        nc.tensor.transpose(small[j][0:E, 0:128], aff[j][:, :], identity[:, :]).then_inc(aff_turned[j], 1)
                pe.wait_ge(numbered, START + 1)
                pe.wait_ge(found, START + 3 * (cap // 8))
                nc.tensor.transpose(small[0][0:cap, 128:128 + E], chosen_f[:, :], identity[0:E, 0:E])
                nc.tensor.transpose(small[0][0:cap, 256:256 + E], chosen[:, :], identity[0:E, 0:E]).then_inc(final_turned, 1)

            @block.vector
            def _(ve):
                ve.wait_ge(squares, START + count)
                nc.vector.tensor_scalar(ssum[:, :], ssum[:, :], 1.0 / D, EPS, ALU.mult, ALU.add).then_inc(mean, 1)
                ve.wait_ge(root, START + 1)
                nc.vector.reciprocal(ssum[:, :], ssum[:, :]).then_inc(inv, 1)
                with ve.Fori(0, count // B) as i:
                    for j in range(B):
                        wait_alone(ve, turned[j], START + i + 1, passed_ve)
                        wait_alone(ve, scored[j], START + i, passed_ve)
                        for k in range(KD):
                            nc.vector.tensor_scalar(hT[j][:, k, :], turnedP[j][:, k, :], cols_a[:, k, col:col + 1], cols_b[:, k, col:col + 1],
                                                    ALU.mult, ALU.add).then_inc(h_ready[j], 1)
                    for j in range(B):
                        wait_alone(ve, scored[j], START + i + 1, passed_ve)
                        wait_alone(ve, raised[j], START + i, passed_ve)
                        nc.vector.tensor_reduce(top[j][:, :], logits[j][:, 0:E], AX.X, ALU.max, negate=True).then_inc(maxed[j], 1)
                    for j in range(B):
                        wait_alone(ve, raised[j], START + i + 1, passed_ve)
                        nc.vector.reciprocal(den[j][:, :], den[j][:, :]).then_inc(inverted[j], 1)
                        wait_alone(ve, inverted[j], START + i + 1, passed_ve)
                        nc.vector.tensor_scalar(aff[j][:, :], aff[j][:, :], den[j][:, 0:1], None, ALU.mult).then_inc(weighed[j], 1)
                    for j in range(B):
                        wait_alone(ve, aff_turned[j], START + i + 1, passed_ve)
                        nc.vector.tensor_copy(affT[:, bass.ds((i * B + j) * 128, 128)], small[j][0:E, 0:128]).then_inc(aff_taken[j], 1)
                for j in range(B):
                    ve.wait_ge(aff_taken[j], START + count // B)
                for r in range(cap // 8):
                    eight = slice(8 * r, 8 * r + 8)
                    if r:
                        ve.wait_ge(found, START + 3 * r)
                    nc.vector.max(chosen[:, eight], affT[:, :]).then_inc(found, 1)
                    ve.wait_ge(found, START + 3 * r + 1)
                    nc.vector.max_index(chosen_at[:, eight], chosen[:, eight], affT[:, :]).then_inc(found, 1)
                    ve.wait_ge(found, START + 3 * r + 2)
                    nc.vector.match_replace(affT[:, :], chosen[:, eight], affT[:, :], -1.0).then_inc(found, 1)
                ve.wait_ge(found, START + 3 * (cap // 8))
                nc.vector.tensor_scalar(chosen_f[:, :], chosen_at[:, :], float(first * 128), None, ALU.add).then_inc(numbered, 1)
                ve.wait_ge(final_turned, START + 1)
                nc.vector.tensor_copy(choice_idx[0:cap, :], small[0][0:cap, 128:128 + E]).then_inc(final_taken, 1)
                nc.vector.tensor_copy(choice_aff[0:cap, :], small[0][0:cap, 256:256 + E]).then_inc(final_taken, 1)
                ve.wait_ge(final_taken, START + 2)


FF = 512
KF = FF // 128


def zero_sums(nc, st, F, tiles):
    zeros = st.sb("zeros", [128, D])
    zeroed, f_zeroed = st.sem("zeroed"), st.sem("f_zeroed")

    def on_scalar(act):
        act.wait_ge(zeroed, START + 1)
        for t in tiles:
            act.dma_start(F[t * 128:(t + 1) * 128, :], zeros[:, :]).then_inc(f_zeroed, 16)
        act.wait_ge(f_zeroed, START + 16 * len(tiles))

    def on_gpsimd(po):
        nc.gpsimd.memset(zeros[:, :], 0.0).then_inc(zeroed, 1)

    return on_scalar, on_gpsimd


def choice_experts(nc, name, XN, F, sets, cols_a, cols_b, w_gate, w_up, w_down, identity):
    E = 16
    B = 2
    NS = len(sets)
    M = sum(s[0] for s in sets)
    at = [0, sets[0][0]]
    with Stage(nc, name) as st:
        sb, ps, sem = st.sb, st.ps, st.sem
        wg = [sb(f"wg{j}", [128, KD, FF]) for j in range(B)]
        wu = [sb(f"wu{j}", [128, KD, FF]) for j in range(B)]
        wd = [sb(f"wd{j}", [128, KF, D]) for j in range(B)]
        idx = [[sb(f"idx{j}_{s}", [sets[s][0], 1], i32) for s in range(NS)] for j in range(B)]
        xg = [[sb(f"xg{j}_{s}", [sets[s][0], D]) for s in range(NS)] for j in range(B)]
        xT = sb("xT", [128, KD, M])
        hid = sb("hid", [128, KF, M])
        ex = [sb(f"ex{j}", [128, M]) for j in range(2)]
        y = [sb(f"y{s}", [sets[s][0], D]) for s in range(NS)]
        turnedP = ps("turned", [128, KD, 128])
        turnedC = ps("turnedC", [128, KD, 32]) if NS > 1 else None
        gu = [ps(f"gu{j}", [128, 2, M]) for j in range(2)]
        acc = [ps(f"acc{j}", [128, 512]) for j in range(3)]
        w_in, idx_ready, down_done = ([sem(f"{n}{j}") for j in range(B)] for n in ("w_in", "idx_ready", "down_done"))
        gathered = [sem(f"gathered{j}", from_zero=True) for j in range(B)]
        summed = sem("summed", from_zero=True)
        turned, x_ready, upped, raised, steps, hid_ready = sem("turned"), sem("x_ready"), sem("upped"), sem("raised"), sem("steps"), sem("hid_ready")
        downed, y_ready, added = sem("downed"), sem("y_ready"), sem("added")
        passed_sp, passed_ve, passed_po, passed_act = sem("passed_sp"), sem("passed_ve"), sem("passed_po"), sem("passed_act")
        YC = 2 * NS
        with nc.Block() as block:
            @block.sync
            def _(sp):
                st.open(sp)
                with sp.Fori(0, E // B) as i:
                    for j in range(B):
                        e = i * B + j
                        wait_alone(sp, down_done[j], START + i, passed_sp)
                        sp.dma_start(wg[j][:, :, :], w_gate[bass.ds(e, 1), :, :].rearrange("e (k p) n -> p (e k) n", p=128)).then_inc(w_in[j], 16)
                        sp.dma_start(wu[j][:, :, :], w_up[bass.ds(e, 1), :, :].rearrange("e (k p) n -> p (e k) n", p=128)).then_inc(w_in[j], 16)
                        sp.dma_start(wd[j][:, :, :], w_down[bass.ds(e, 1), :, :].rearrange("e (k p) n -> p (e k) n", p=128)).then_inc(w_in[j], 16)

            @block.gpsimd
            def _(po):
                with po.Fori(0, E // B) as i:
                    def gather(j):
                        wait_alone(po, idx_ready[j], START + (i + 1) * NS, passed_po)
                        wait_alone(po, turned, START + (i * B), passed_po)
                        for s in range(NS):
                            po.indirect_dma_start(xg[j][s][:, :], None, XN, bass.IndirectOffsetOnAxis(ap=idx[j][s][:, :], axis=0)).then_inc(gathered[j], 16)

                    gather(0)
                    gather(1)
                    for j in range(B):
                        e = i * B + j
                        wait_alone(po, y_ready, START + (e + 1) * YC, passed_po)
                        for s in range(NS):
                            po.indirect_dma_start(F, bass.IndirectOffsetOnAxis(ap=idx[j][s][:, :], axis=0), y[s][:, :], None,
                                                  compute_op=ALU.add).then_inc(summed, 16)
                        wait_alone(po, summed, (e + 1) * 16 * NS, added)

            @block.scalar
            def _(act):
                with act.Fori(0, E // B) as i:
                    for j in range(B):
                        e = i * B + j
                        for f in range(KF):
                            act.wait_ge(upped, START + e * KF + f + 1)
                            act.wait_ge(steps, START + (e * KF + max(f - 1, 0)) * 4)
                            nc.scalar.activation(ex[f % 2][:, :], gu[f % 2][:, 0, :], ACT.Exp, scale=-1.0).then_inc(raised, 1)
                        act.wait_ge(added, START + e)
                        for c in range(YC):
                            s = c // 2
                            act.wait_ge(downed, START + e * YC + c + 1)
                            act.sem_inc(passed_act, 1)
                            nc.scalar.activation(y[s][:, (c % 2) * 512:(c % 2 + 1) * 512], acc[c % 3 if NS == 1 else c % 3][0:sets[s][0], :], ACT.Copy,
                                                 scale=sets[s][5][0:sets[s][0], bass.ds(e, 1)]).then_inc(y_ready, 1)

            @block.tensor
            def _(pe):
                with pe.Fori(0, E // B) as i:
                    for j in range(B):
                        e = i * B + j
                        pe.wait_ge(gathered[j], (i + 1) * 16 * NS)
                        pe.wait_ge(x_ready, START + e * KD * NS)
                        for k in range(KD):
                            tp = nc.tensor.transpose(turnedP[:, k, 0:sets[0][0]], xg[j][0][:, k * 128:(k + 1) * 128], identity[0:sets[0][0], 0:sets[0][0]])
                            if NS > 1:
                                tp = nc.tensor.transpose(turnedC[:, k, :], xg[j][1][:, k * 128:(k + 1) * 128], identity[0:sets[1][0], 0:sets[1][0]])
                        tp.then_inc(turned, 1)
                        pe.wait_ge(x_ready, START + (e + 1) * KD * NS)
                        pe.wait_ge(w_in[j], START + (i + 1) * 48)
                        for f in range(KF):
                            pe.wait_ge(steps, START + (e * KF + max(f - 1, 0)) * 4)
                            for h, w in enumerate((wg, wu)):
                                for k in range(KD):
                                    mm = nc.tensor.matmul(gu[f % 2][:, h, :], w[j][:, k, f * 128:(f + 1) * 128], xT[:, k, :],
                                                          start=(k == 0), stop=(k == KD - 1))
                            mm.then_inc(upped, 1)
                        pe.wait_ge(steps, START + (e + 1) * KF * 4)
                        for c in range(YC):
                            s = c // 2
                            pe.wait_ge(y_ready, START + e * YC + max(c - 2, 0))
                            for f in range(KF):
                                mm = nc.tensor.matmul(acc[c % 3][0:sets[s][0], :], hid[:, f, at[s]:at[s] + sets[s][0]],
                                                      wd[j][:, f, (c % 2) * 512:(c % 2 + 1) * 512], start=(f == 0), stop=(f == KF - 1))
                            mm.then_inc(downed, 1)
                        pe.wait_ge(downed, START + (e + 1) * YC)
                        pe.sem_inc(down_done[j], 1)

            @block.vector
            def _(ve):
                with ve.Fori(0, E // B) as i:
                    wait_alone(ve, added, START + i * B, passed_ve)
                    for j in range(B):
                        for s in range(NS):
                            nc.vector.tensor_copy(idx[j][s][:, :], sets[s][4][0:sets[s][0], bass.ds(i * B + j, 1)]).then_inc(idx_ready[j], 1)
                    for j in range(B):
                        e = i * B + j
                        wait_alone(ve, turned, START + e + 1, passed_ve)
                        wait_alone(ve, upped, START + e * KF, passed_ve)
                        for k in range(KD):
                            for s in range(NS):
                                cap, _, _, col, _, _ = sets[s]
                                src = turnedP[:, k, 0:cap] if s == 0 else turnedC[:, k, :]
                                nc.vector.tensor_scalar(xT[:, k, at[s]:at[s] + cap], src, cols_a[:, k, col:col + 1], cols_b[:, k, col:col + 1],
                                                        ALU.mult, ALU.add).then_inc(x_ready, 1)
                        for f in range(KF):
                            base = (e * KF + f) * 4
                            wait_alone(ve, raised, START + e * KF + f + 1, passed_ve)
                            wait_alone(ve, downed, START + e * YC, passed_ve)
                            nc.vector.tensor_scalar(ex[f % 2][:, :], ex[f % 2][:, :], 1.0, None, ALU.add).then_inc(steps, 1)
                            wait_alone(ve, steps, START + base + 1, passed_ve)
                            nc.vector.reciprocal(ex[f % 2][:, :], ex[f % 2][:, :]).then_inc(steps, 1)
                            wait_alone(ve, steps, START + base + 2, passed_ve)
                            nc.vector.tensor_tensor(ex[f % 2][:, :], ex[f % 2][:, :], gu[f % 2][:, 0, :], ALU.mult).then_inc(steps, 1)
                            wait_alone(ve, steps, START + base + 3, passed_ve)
                            nc.vector.tensor_tensor(hid[:, f, :], ex[f % 2][:, :], gu[f % 2][:, 1, :], ALU.mult).then_inc(steps, 1)


def add_gated(nc, name, F, gate, first, count, X):
    B = 2
    with Stage(nc, name) as st:
        sb, sem = st.sb, st.sem
        gt = sb("gt", [128, D])
        f = [sb(f"f{j}", [128, D]) for j in range(B)]
        g_in = sem("g_in")
        f_in, gated, added = ([sem(f"{n}{j}") for j in range(B)] for n in ("f_in", "gated", "added"))
        passed_sp, passed_ve = sem("passed_sp"), sem("passed_ve")
        with nc.Block() as block:
            @block.sync
            def _(sp):
                st.open(sp)
                sp.dma_start(gt[:, :], gate.partition_broadcast(128)).then_inc(g_in, 16)
                with sp.Fori(0, count // B) as i:
                    for j in range(B):
                        wait_alone(sp, added[j], START + i, passed_sp)
                        sp.dma_start(f[j][:, :], F[bass.ds((first + i * B + j) * 128, 128), :]).then_inc(f_in[j], 16)

            @block.vector
            def _(ve):
                ve.wait_ge(g_in, START + 16)
                with ve.Fori(0, count // B) as i:
                    for j in range(B):
                        wait_alone(ve, f_in[j], START + (i + 1) * 16, passed_ve)
                        nc.vector.tensor_tensor(f[j][:, :], f[j][:, :], gt[:, :], ALU.mult).then_inc(gated[j], 1)
                        wait_alone(ve, gated[j], START + i + 1, passed_ve)
                        xt = X[:, bass.ds(first + i * B + j, 1), :].rearrange("p a n -> p (a n)")
                        nc.vector.tensor_tensor(xt, xt, f[j][:, :], ALU.add).then_inc(added[j], 1)
                for j in range(B):
                    ve.wait_ge(added[j], START + count // B)


def final_norm(nc, name, X, gain, out=None):
    B = 2
    with Stage(nc, name) as st:
        sb, sem = st.sb, st.sem
        gt = sb("gt", [128, D])
        ssum = sb("ssum", [128, LAT_TILES])
        junk = sb("junk", [128, D])
        g_in, squares, mean, root, inv, scaled, stored = (sem(n) for n in ("g_in", "squares", "mean", "root", "inv", "scaled", "stored"))
        with nc.Block() as block:
            @block.sync
            def _(sp):
                st.open(sp)
                sp.dma_start(gt[:, :], gain.partition_broadcast(128)).then_inc(g_in, 16)
                if out is not None:
                    for t in range(LAT_TILES):
                        sp.wait_ge(scaled, START + t + 1)
                        sp.dma_start(out[t * 128:(t + 1) * 128, :], X[:, CTX_TILES + t, :]).then_inc(stored, 16)
                    sp.wait_ge(stored, START + LAT_TILES * 16)

            @block.scalar
            def _(act):
                for t in range(LAT_TILES):
                    if t:
                        act.wait_ge(squares, START + t)
                    nc.scalar.activation(junk[:, :], X[:, CTX_TILES + t, :], ACT.Square, accum_out=ssum[:, t:t + 1]).then_inc(squares, 1)
                act.wait_ge(mean, START + 1)
                nc.scalar.activation(ssum[:, :], ssum[:, :], ACT.Sqrt).then_inc(root, 1)

            @block.vector
            def _(ve):
                ve.wait_ge(squares, START + LAT_TILES)
                nc.vector.tensor_scalar(ssum[:, :], ssum[:, :], 1.0 / D, EPS, ALU.mult, ALU.add).then_inc(mean, 1)
                ve.wait_ge(root, START + 1)
                nc.vector.reciprocal(ssum[:, :], ssum[:, :]).then_inc(inv, 1)
                ve.wait_ge(inv, START + 1)
                ve.wait_ge(g_in, START + 16)
                for t in range(LAT_TILES):
                    xt = X[:, CTX_TILES + t, :]
                    nc.vector.scalar_tensor_tensor(xt, xt, ssum[:, t:t + 1], gt[:, :], ALU.mult, ALU.mult).then_inc(scaled, 1)
                ve.wait_ge(scaled, START + LAT_TILES)


def first_block(nc, t, X, identity, scratch):
    with ExitStack() as own:
        def keep(name, shape, dt=fp32):
            return own.enter_context(nc.sbuf_tensor(name, shape, dt))

        cols = keep("cols", [128, 4, KD, 2])
        lat_idx, ctx_idx = keep("lat_idx", [128, 16], i32), keep("ctx_idx", [32, 16], i32)
        lat_aff, ctx_aff = keep("lat_aff", [128, 16]), keep("ctx_aff", [32, 16])
        gates, P1, RT, V, Z, mix, XN, F = (scratch[n] for n in ("gates", "P1", "RT", "V", "Z", "mix", "XN", "F"))
        for l in range(DEPTH):
            n = f"l{l}"
            both = l < DEPTH - 1
            modulation(nc, n + "mod", t["c"][0], t["c_ctx"], t["ada_w"][l], t["ada_b"][l], t["norm1_g"][l], t["norm2_g"][l], cols, gates, identity,
                       lambda st: zero_sums(nc, st, F, range(0 if both else CTX_TILES, TILES)))
            project(nc, n + "proj", X, cols[:, 0, :, :], cols[:, 1, :, :], t["w_in"][l], IN1, IN1 // 4, P1, identity)
            heads_first(nc, n + "heads", P1, t["rope1"], t["mla_w_uq"][l], t["mla_w_ukv"][l], t["mla_q_norm_g"][l], t["mla_kv_norm_g"][l],
                        RT, V, Z, identity)
            mla_attention(nc, n + "mla", RT, V, mix, identity, both)
            swa_attention(nc, n + "swa", RT, P1, mix, t["window"], t["swa_sink"][l], identity, both)
            mix_out(nc, n + "out", CTX_TILES, LAT_TILES, mix, t["w_o"][l], gates[0, 2 * D:3 * D], X, identity, (P1, Z, t["conv_w"][l], 3))
            if both:
                mix_out(nc, n + "outc", 0, CTX_TILES, mix, t["w_o"][l], gates[1, 2 * D:3 * D], X, identity, (P1, Z, t["conv_w"][l], 1))
            a2, b2 = cols[:, 2, :, :], cols[:, 3, :, :]
            route_choice(nc, n + "route", CTX_TILES, LAT_TILES, X, a2, b2, 0, t["router_w"][l], XN, 128, lat_idx, lat_aff, identity)
            sets = [(128, CTX, SEQ, 0, lat_idx, lat_aff)]
            if both:
                route_choice(nc, n + "routec", 0, CTX_TILES, X, a2, b2, 1, t["router_w"][l], XN, 32, ctx_idx, ctx_aff, identity)
                sets.append((32, 0, CTX, 1, ctx_idx, ctx_aff))
            choice_experts(nc, n + "exp", XN, F, sets, a2, b2, t["exp_w_gate"][l], t["exp_w_up"][l], t["exp_w_down"][l], identity)
            add_gated(nc, n + "add", F, gates[0, 5 * D:6 * D], CTX_TILES, LAT_TILES, X)
            if both:
                add_gated(nc, n + "addc", F, gates[1, 5 * D:6 * D], 0, CTX_TILES, X)


A_HEADS, A_DK, A_DV = 4, 64, 128
G_HEADS, G_DK, G_DV, G_RANK = 4, 32, 64, 16
N_HEADS, N_DK = 4, 64
GRID, N_ROWS, N_COLS = 64, 8, 16
I_QA, I_VA = 0, 2 * A_HEADS * 2 * A_DK
I_QB = I_VA + A_HEADS * A_DV
I_VB = I_QB + 2 * G_HEADS * G_DK
I_RB = I_VB + G_HEADS * G_DV
I_GB = I_RB + G_HEADS * G_DV
I_QN = I_GB + 2 * G_RANK
I_VN = I_QN + 2 * N_HEADS * N_DK
IN2 = I_VN + N_HEADS * N_DK
T_QA, T_KA = 0, A_HEADS * 2 * A_DK
T_QN = 2 * T_KA
T_KN = T_QN + N_HEADS * N_DK
T_QB = T_KN + N_HEADS * N_DK
T_KB = T_QB + G_HEADS * G_DK
T_GB = T_KB + G_HEADS * G_DK
R2 = T_GB + 2 * G_RANK
LAMBDA_START = 0.8 - 0.6


def heads_second(nc, name, P2, table, RT, identity):
    B = 2
    FULL = R2 // 128
    rest = R2 - FULL * 128
    NH = 2 * A_HEADS * 2
    chunks = [(None, c) for c in range(T_QN // 128)] + [(I_QN + 128 * c, None) for c in range(4)] + [(I_QB + 128 * c, None) for c in range(2)]
    with Stage(nc, name) as st:
        sb, ps, sem = st.sb, st.ps, st.sem
        p = [sb(f"p{j}", [128, IN2]) for j in range(B)]
        tab = [sb(f"tab{j}", [128, 128]) for j in range(B)]
        row = [sb(f"row{j}", [128, NH, A_DK]) for j in range(B)]
        swp = [sb(f"swp{j}", [128, NH, A_DK]) for j in range(B)]
        rT = [sb(f"rT{j}", [128, FULL + 1, 128]) for j in range(B)]
        tr = [ps(f"tr{j}", [128, 16, 128]) for j in range(B)]
        p_in, rotated, turned, taken_a, taken_v, stored = ([sem(f"{n}{j}") for j in range(B)] for n in
                                                           ("p_in", "rotated", "turned", "taken_a", "taken_v", "stored"))
        passed_sp, passed_ve = sem("passed_sp"), sem("passed_ve")
        rtv = RT[0:FULL * 128, :].rearrange("(k p) n -> p k n", p=128)
        with nc.Block() as block:
            @block.sync
            def _(sp):
                st.open(sp)
                with sp.Fori(0, TILES // B) as i:
                    for j in range(B):
                        n = i * B + j
                        wait_alone(sp, turned[j], START + i, passed_sp)
                        sp.dma_start(p[j][:, :], P2[bass.ds(n * 128, 128), :]).then_inc(p_in[j], 16)
                        sp.dma_start(tab[j][:, :], table[bass.ds(n * 128, 128), :]).then_inc(p_in[j], 16)
                    for j in range(B):
                        n = i * B + j
                        wait_alone(sp, taken_a[j], START + (i + 1) * 2, passed_sp)
                        wait_alone(sp, taken_v[j], START + (i + 1) * 3, passed_sp)
                        sp.dma_start(rtv[:, :, bass.ds(n * 128, 128)], rT[j][:, 0:FULL, :]).then_inc(stored[j], 16)
                        sp.dma_start(RT[T_GB:R2, bass.ds(n * 128, 128)], rT[j][0:rest, FULL, :]).then_inc(stored[j], 16)
                for j in range(B):
                    sp.wait_ge(stored[j], START + TILES // B * 32)

            @block.tensor
            def _(pe):
                with pe.Fori(0, TILES // B) as i:
                    for j in range(B):
                        pe.wait_ge(rotated[j], START + (i + 1) * 4)
                        pe.wait_ge(taken_a[j], START + i * 2)
                        pe.wait_ge(taken_v[j], START + i * 3)
                        flat = row[j][:, :, :].rearrange("p h d -> p (h d)")
                        for c, (col, own) in enumerate(chunks):
                            src = flat[:, own * 128:own * 128 + 128] if col is None else p[j][:, col:col + 128]
                            nc.tensor.transpose(tr[j][:, c, :], src, identity[:, :])
                        nc.tensor.transpose(tr[j][0:rest, FULL, :], p[j][:, I_GB:I_GB + rest], identity[:, :]).then_inc(turned[j], 1)

            @block.scalar
            def _(act):
                with act.Fori(0, TILES // B) as i:
                    for j in range(B):
                        act.wait_ge(turned[j], START + i + 1)
                        act.wait_ge(stored[j], START + i * 32)
                        for g in (0, 8):
                            nc.scalar.activation(rT[j][:, g:g + 4, :], tr[j][:, g:g + 4, :], ACT.Copy).then_inc(taken_a[j], 1)

            @block.vector
            def _(ve):
                with ve.Fori(0, TILES // B) as i:
                    for j in range(B):
                        wait_alone(ve, p_in[j], START + (i + 1) * 32, passed_ve)
                        wait_alone(ve, turned[j], START + i, passed_ve)
                        wait_alone(ve, rotated[j], START + i * 4, passed_ve)
                        x = p[j][:, 0:I_VA].rearrange("p (h d) -> p h d", d=A_DK)
                        cosines = tab[j][:, 0:64].unsqueeze(1).broadcast_to([128, NH, A_DK])
                        nc.vector.tensor_tensor(row[j][:, :, :], x, cosines, ALU.mult).then_inc(rotated[j], 1)
                        for half in range(2):
                            lo, hi = half * 32, half * 32 + 32
                            xs = x[:, :, lo:hi].rearrange("p h (a d) -> p h a d", a=2)[:, :, ::-1, :]
                            sines = tab[j][:, 64 + lo:64 + hi].rearrange("p (a d) -> p a d", a=2).unsqueeze(1).broadcast_to([128, NH, 2, 16])
                            nc.vector.tensor_tensor(swp[j][:, :, lo:hi].rearrange("p h (a d) -> p h a d", a=2), xs, sines, ALU.mult).then_inc(rotated[j], 1)
                        wait_alone(ve, rotated[j], START + i * 4 + 3, passed_ve)
                        nc.vector.tensor_tensor(row[j][:, :, :], row[j][:, :, :], swp[j][:, :, :], ALU.add).then_inc(rotated[j], 1)
                    for j in range(B):
                        wait_alone(ve, turned[j], START + i + 1, passed_ve)
                        wait_alone(ve, stored[j], START + i * 32, passed_ve)
                        nc.vector.tensor_copy(rT[j][:, 4:8, :], tr[j][:, 4:8, :]).then_inc(taken_v[j], 1)
                        nc.vector.tensor_copy(rT[j][:, 12:14, :], tr[j][:, 12:14, :]).then_inc(taken_v[j], 1)
                        nc.vector.tensor_copy(rT[j][0:rest, FULL, :], tr[j][0:rest, FULL, :]).then_inc(taken_v[j], 1)


def diff_attention(nc, name, RT, P2, OD, identity):
    units = [(CTX + 128 * t, [(0, ROWS)], None) for t in range(LAT_TILES)]
    vv = P2.rearrange("(t p) n -> p t n", p=128)
    attend(nc, name, A_HEADS, 2, A_DK, A_DV, A_DK ** -0.5,
           lambda it, a: RT[bass.ds((it * 2 + a) * A_DK + T_QA, A_DK), :],
           lambda it, a: RT[bass.ds((it * 2 + a) * A_DK + T_KA, A_DK), :],
           lambda it, a: vv[:, :, bass.ds(it * A_DV + I_VA, A_DV)],
           False, True, units, lambda it, a, row: OD[row:row + 128, bass.ds((it * 2 + a) * A_DV, A_DV)], identity)


PATTERNS = 5
BAND = 10 * GRID


def neighbourhood_bias(nc, st, rpb, mask, padded, BT):
    W = N_HEADS * 19 * 127
    rep = st.sb("rep", [GRID, N_HEADS, 19, 127])
    mk = st.sb("mk", [128, PATTERNS * BAND])
    bt = [st.sb(f"bt{j}", [128, PATTERNS * BAND]) for j in range(2)]
    zeroed, cleared, placed, mask_in, added, bias_stored = (st.sem(n) for n in ("zeroed", "cleared", "placed", "mask_in", "added", "bias_stored"))
    bias_in = [st.sem(f"bias_in{h}") for h in range(N_HEADS)]

    def on_scalar(act):
        act.dma_start(mk[:, :], mask).then_inc(mask_in, 16)
        act.wait_ge(zeroed, START + 1)
        for h in range(N_HEADS):
            inner = rep[:, h, 2:2 + 2 * N_ROWS - 1, 48:48 + 2 * N_COLS - 1]
            act.dma_start(inner, rpb[h].partition_broadcast(GRID)).then_inc(cleared, 16)
        act.wait_ge(cleared, START + 16 * N_HEADS)
        act.dma_start(padded.rearrange("q h r c -> q (h r c)"), rep[:, :, :, :].rearrange("q h r c -> q (h r c)")).then_inc(placed, 16)
        act.wait_ge(placed, START + 16)
        for h in range(N_HEADS):
            if h >= 2:
                act.wait_ge(bias_stored, START + 16 * (h - 1))
            for pat in range(PATTERNS):
                for a in range(2):
                    src = dram_view(padded.tensor, h * 19 * 127 + (9 - 2 * pat - a) * 127 + 63, [[W - 1, 64], [127, 10], [1, 64]])
                    dst = bt[h % 2][64 * a:64 * a + 64, pat * BAND:(pat + 1) * BAND].rearrange("p (r c) -> p r c", c=GRID)
                    act.dma_start(dst, src).then_inc(bias_in[h], 16)
            if h:
                act.wait_ge(added, START + h)
                act.wait_ge(bias_stored, START + 16 * (h - 1))
                act.dma_start(BT[h - 1], bt[(h - 1) % 2][:, :]).then_inc(bias_stored, 16)
        act.wait_ge(added, START + N_HEADS)
        act.wait_ge(bias_stored, START + 16 * (N_HEADS - 1))
        act.dma_start(BT[N_HEADS - 1], bt[(N_HEADS - 1) % 2][:, :]).then_inc(bias_stored, 16)
        act.wait_ge(bias_stored, START + 16 * N_HEADS)

    def on_gpsimd(po):
        nc.gpsimd.memset(rep[:, :, :, :], 0.0).then_inc(zeroed, 1)
        po.wait_ge(mask_in, START + 16)
        for h in range(N_HEADS):
            po.wait_ge(bias_in[h], START + 160)
            nc.gpsimd.tensor_tensor(bt[h % 2][:, :], bt[h % 2][:, :], mk[:, :], ALU.add).then_inc(added, 1)

    return on_scalar, on_gpsimd


def neighbourhood_attention(nc, name, RT, P2, BT, mix, identity):
    units = []
    for t in range(LAT_TILES):
        start = min(max(2 * t - 4, 0), SEQ // GRID - 10)
        units.append((CTX + 128 * t, [(0, CTX), (CTX + start * GRID, BAND)], ((2 * t - start) // 2 * BAND, BAND)))
    vv = P2.rearrange("(t p) n -> p t n", p=128)
    base = A_HEADS * A_DV + G_HEADS * G_DV
    attend(nc, name, N_HEADS // 2, 2, N_DK, N_DK, N_DK ** -0.5,
           lambda it, a: RT[bass.ds((it * 2 + a) * N_DK + T_QN, N_DK), :],
           lambda it, a: RT[bass.ds((it * 2 + a) * N_DK + T_KN, N_DK), :],
           lambda it, a: vv[:, :, bass.ds((it * 2 + a) * N_DK + I_VN, N_DK)],
           False, False, units, lambda it, a, row: mix[row:row + 128, bass.ds((it * 2 + a) * N_DK + base, N_DK)], identity,
           bias_of=lambda it, a: BT[bass.ds(it * 2 + a, 1)].rearrange("h p n -> p (h n)"))


def gated_scan(nc, name, backward, RT, P2, w_dec, b_dec, masks, block_mask, OG, blank, identity):
    CH = 128
    W = G_HEADS * G_DV
    levels = [64, 32, 16, 8, 4, 2, 1, 0]
    first = CTX_TILES
    order = (list(range(CTX_TILES))[::-1] + list(range(CTX_TILES, TILES))[::-1]) if backward else list(range(TILES))
    LT = LAT_TILES
    with Stage(nc, name) as st:
        sb, ps, sem = st.sb, st.ps, st.sem
        q, k = sb("q", [128, ROWS]), sb("k", [128, ROWS])
        low = sb("low", [G_RANK, ROWS])
        wd = sb("wd", [G_RANK, 128])
        bd = sb("bd", [128, 1])
        v = sb("v", [128, TILES, W])
        zb, t1, t2 = sb("zb", [128, ROWS]), sb("t1", [128, ROWS]), sb("t2", [128, ROWS])
        keep, b = sb("keep", [128, ROWS]), sb("b", [128, ROWS])
        ql = [sb(f"ql{j}", [128, LT, G_HEADS, CH]) for j in range(2)]
        kl = [sb(f"kl{j}", [128, SEQ]) for j in range(2)]
        eq, ek = [sb(f"eq{j}", [128, SEQ // 2]) for j in range(2)], [sb(f"ek{j}", [128, SEQ // 2]) for j in range(2)]
        mk = sb("mk", [128, 8, CH], i32)
        bm = sb("bm", [128, W])
        A = sb("A", [128, LT, G_HEADS, CH])
        qb, kb = sb("qb", [128, ROWS]), sb("kb", [128, ROWS])
        decay = sb("decay", [128, TILES])
        kbT = [sb(f"kbT{j}", [128, 128]) for j in range(2)]
        S = sb("S", [128, W])
        um = sb("um", [128, W])
        o = [sb(f"o{j}", [128, W]) for j in range(2)]
        z = ps("z", [128, 3, 512])
        pa = [ps(f"pa{j}", [128, G_HEADS, CH]) for j in range(2)]
        po_ = ps("po", [128, 512])
        pu = ps("pu", [128, 512])
        pk = ps("pk", [128, 512])
        zeros = sb("zeros", [128, D])
        zeroed, blanked = sem("zeroed"), sem("blanked")
        loaded, zed, gate, cumulated = sem("loaded"), sem("zed"), sem("gate"), sem("cumulated")
        exped, level_diff, level_exp, level_ready, scored, picked = (sem(n) for n in ("exped", "level_diff", "level_exp", "level_ready", "scored", "picked"))
        ends, ends_exp, ends_ready = sem("ends"), sem("ends_exp"), sem("ends_ready")
        turned, turn_taken, updated, mixed, state, out_taken, stored = (sem(n) for n in
                                                                        ("turned", "turn_taken", "updated", "mixed", "state", "out_taken", "stored"))
        NF = G_HEADS + 1
        spans = [(0, 512), (512, 512), (1024, 256)]

        def halves(x, L, off=0):
            xv = x[:, off:off + SEQ].rearrange("p (n l) -> p n l", l=2 * L)
            lo, hi = xv[:, :, 0:L], xv[:, :, L:2 * L]
            if backward:
                return lo, hi, xv[:, :, L:L + 1]
            return hi, lo, xv[:, :, L - 1:L]

        with nc.Block() as block:
            @block.sync
            def _(sp):
                st.open(sp)
                d = 1 if backward else 0
                sp.dma_start(low[:, :], RT[T_GB + d * G_RANK:T_GB + (d + 1) * G_RANK, :]).then_inc(loaded, 16)
                sp.dma_start(wd[:, :], w_dec[d]).then_inc(loaded, 16)
                sp.dma_start(bd[:, :], b_dec[d].rearrange("(p a) -> p a", a=1)).then_inc(loaded, 16)
                sp.dma_start(q[:, :], RT[T_QB:T_QB + 128, :]).then_inc(loaded, 16)
                sp.dma_start(k[:, :], RT[T_KB:T_KB + 128, :]).then_inc(loaded, 16)
                sp.dma_start(v[:, :, :], P2[:, I_VB:I_RB].rearrange("(t p) n -> p t n", p=128)).then_inc(loaded, 16)
                sp.dma_start(mk[:, :, :], masks).then_inc(loaded, 16)
                sp.dma_start(bm[:, :], block_mask).then_inc(loaded, 16)
                sp.wait_ge(zeroed, START + 1)
                for rows in blank:
                    sp.dma_start(rows, zeros[:, :]).then_inc(blanked, 16)
                n = 0
                for c in order:
                    if c >= first:
                        sp.wait_ge(out_taken, START + n + 1)
                        sp.wait_ge(stored, START + 16 * n)
                        sp.dma_start(OG[c * 128:(c + 1) * 128, :], o[n % 2][:, :]).then_inc(stored, 16)
                        n += 1
                sp.wait_ge(stored, START + 16 * n)
                sp.wait_ge(blanked, START + 16 * len(blank))

            @block.tensor
            def _(pe):
                pe.wait_ge(loaded, START + 128)
                for n, (s, m) in enumerate(spans):
                    mm = nc.tensor.matmul(z[:, n, 0:m], wd[:, :], low[:, s:s + m], start=True, stop=True)
                mm.then_inc(zed, 1)
                n = 0
                for lv, L in enumerate(levels):
                    pe.wait_ge(level_ready, START + NF * (lv + 1))
                    for c in range(LT):
                        if n >= 2:
                            pe.wait_ge(picked, START + n - 1)
                        nc.tensor.matmul(pa[n % 2][:, :, :], kl[lv % 2][:, c * CH:(c + 1) * CH], ql[lv % 2][:, c, :, :],
                                         start=True, stop=True).then_inc(scored, 1)
                        n += 1
                pe.wait_ge(ends_ready, START + 2)
                pe.wait_ge(picked, START + n)
                outs = 0
                for i, c in enumerate(order):
                    rows = slice(c * CH, (c + 1) * CH)
                    if i:
                        pe.wait_ge(turn_taken, START + i)
                    nc.tensor.transpose(pk[:, 0:128], kb[:, rows], identity[:, :]).then_inc(turned, 1)
                    pe.wait_ge(state, START + 1 + 2 * i)
                    if c >= first:
                        if outs:
                            pe.wait_ge(out_taken, START + outs)
                        nc.tensor.matmul(po_[:, 0:W], qb[:, rows], S[:, :], start=True, stop=False, skip_group_check=True)
                        for h in range(G_HEADS):
                            mm = nc.tensor.matmul(po_[:, h * G_DV:(h + 1) * G_DV], A[:, c - first, h, :], v[:, c, h * G_DV:(h + 1) * G_DV],
                                                  start=False, stop=(h == G_HEADS - 1), skip_group_check=True)
                        mm.then_inc(mixed, 1)
                        outs += 1
                    pe.wait_ge(turn_taken, START + i + 1)
                    nc.tensor.matmul(pu[:, 0:W], kbT[i % 2][:, :], v[:, c, :], start=True, stop=True).then_inc(updated, 1)

            @block.scalar
            def _(act):
                act.wait_ge(gate, START + 1)
                nc.scalar.activation(t1[:, :], zb[:, :], ACT.Abs).then_inc(exped, 1)
                act.wait_ge(exped, START + 1)
                nc.scalar.activation(t1[:, :], t1[:, :], ACT.Exp, scale=-1.0).then_inc(exped, 1)
                act.wait_ge(gate, START + 2)
                nc.scalar.activation(t1[:, :], t1[:, :], ACT.Ln).then_inc(exped, 1)
                act.wait_ge(ends, START + 1)
                nc.scalar.activation(t1[:, :], b[:, :], ACT.Exp).then_inc(ends_exp, 1)
                nc.scalar.activation(t2[:, :], t2[:, :], ACT.Exp).then_inc(ends_exp, 1)
                last = b[:, 0:ROWS:CH] if backward else b[:, CH - 1:ROWS:CH]
                nc.scalar.activation(decay[:, :], last, ACT.Exp).then_inc(ends_exp, 1)
                for lv, L in enumerate(levels):
                    if L:
                        act.wait_ge(level_diff, START + 2 * (lv + 1))
                        nc.scalar.activation(eq[lv % 2][:, :], eq[lv % 2][:, :], ACT.Exp).then_inc(level_exp, 1)
                        nc.scalar.activation(ek[lv % 2][:, :], ek[lv % 2][:, :], ACT.Exp).then_inc(level_exp, 1)

            @block.gpsimd
            def _(po):
                nc.gpsimd.memset(zeros[:, :], 0.0).then_inc(zeroed, 1)
                nc.gpsimd.memset(keep[:, :], 1.0).then_inc(cumulated, 1)
                po.wait_ge(cumulated, START + 1)
                starts = keep[:, CH - 1:ROWS:CH] if backward else keep[:, 0:ROWS:CH]
                nc.gpsimd.memset(starts, 0.0).then_inc(cumulated, 1)
                nc.gpsimd.memset(S[:, :], 0.0).then_inc(state, 1)
                nc.gpsimd.memset(A[:, :, :, :], 0.0).then_inc(cumulated, 1)
                for j in range(2):
                    nc.gpsimd.memset(ql[j][:, :, :, :], 0.0).then_inc(cumulated, 1)
                    nc.gpsimd.memset(kl[j][:, :], 0.0).then_inc(cumulated, 1)

            @block.vector
            def _(ve):
                V_ = nc.vector
                ve.wait_ge(zed, START + 1)
                zf = z[:, :, :].rearrange("p a n -> p (a n)")[:, 0:ROWS]
                V_.tensor_scalar(zb[:, :], zf, bd[:, 0:1], None, ALU.add).then_inc(gate, 1)
                ve.wait_ge(exped, START + 2)
                V_.tensor_scalar(t1[:, :], t1[:, :], 1.0, None, ALU.add).then_inc(gate, 1)
                ve.wait_ge(gate, START + 2)
                V_.tensor_scalar(zb[:, :], zb[:, :], 0.0, 1.0 / 16, ALU.min, ALU.mult).then_inc(gate, 1)
                ve.wait_ge(gate, START + 3)
                ve.wait_ge(exped, START + 3)
                V_.scalar_tensor_tensor(zb[:, :], t1[:, :], -1.0 / 16, zb[:, :], ALU.mult, ALU.add).then_inc(gate, 1)
                ve.wait_ge(gate, START + 4)
                ve.wait_ge(cumulated, START + 7)
                rev = slice(None, None, -1) if backward else slice(None)
                V_.tensor_tensor_scan(b[:, rev], keep[:, rev], zb[:, rev], 0.0, ALU.mult, ALU.add).then_inc(gate, 1)
                V_.tensor_scalar(q[:, :], q[:, :], G_DK ** -0.5, None, ALU.mult).then_inc(gate, 1)
                ve.wait_ge(gate, START + 6)
                bv = b[:, :].rearrange("p (c l) -> p c l", l=CH)
                end = (bv[:, :, 0:1] if backward else bv[:, :, CH - 1:CH]).broadcast_to([128, TILES, CH])
                V_.tensor_tensor(t2[:, :].rearrange("p (c l) -> p c l", l=CH), end, bv, ALU.subtract).then_inc(ends, 1)
                ve.wait_ge(ends_exp, START + 2)
                V_.tensor_tensor(qb[:, :], q[:, :], t1[:, :], ALU.mult).then_inc(ends_ready, 1)
                V_.tensor_tensor(kb[:, :], k[:, :], t2[:, :], ALU.mult).then_inc(ends_ready, 1)

                def differences(lv):
                    L = levels[lv]
                    if not L:
                        return
                    bq, bk, edge = halves(b, L, CTX)
                    n = SEQ // (2 * L)
                    e = edge.broadcast_to([128, n, L])
                    if lv >= 2:
                        ve.wait_ge(level_ready, START + NF * (lv - 1))
                    V_.tensor_tensor(eq[lv % 2][:, :].rearrange("p (n l) -> p n l", l=L), bq, e, ALU.subtract).then_inc(level_diff, 1)
                    V_.tensor_tensor(ek[lv % 2][:, :].rearrange("p (n l) -> p n l", l=L), e, bk, ALU.subtract).then_inc(level_diff, 1)

                def factors(lv):
                    L = levels[lv]
                    if lv >= 2:
                        ve.wait_ge(scored, START + (lv - 1) * LT)
                    if L:
                        ve.wait_ge(level_exp, START + 2 * (lv + 1))
                    for h in range(G_HEADS):
                        rows = slice(h * G_DK, (h + 1) * G_DK)
                        if L:
                            dst = ql[lv % 2][rows, :, h, :].rearrange("p c (n l) -> p c n l", l=2 * L)
                            dst = dst[:, :, :, 0:L] if backward else dst[:, :, :, L:2 * L]
                            qs, _, _ = halves(q[rows, :], L, CTX)
                            V_.tensor_tensor(dst, qs.rearrange("p (c n) l -> p c n l", c=LT),
                                             eq[lv % 2][rows, :].rearrange("p (c n l) -> p c n l", c=LT, l=L), ALU.mult).then_inc(level_ready, 1)
                        else:
                            V_.tensor_copy(ql[lv % 2][rows, :, h, :], q[rows, CTX:ROWS].rearrange("p (c l) -> p c l", c=LT)).then_inc(level_ready, 1)
                    if L:
                        _, kk, _ = halves(kl[lv % 2], L)
                        _, ks, _ = halves(k, L, CTX)
                        V_.tensor_tensor(kk, ks, ek[lv % 2][:, :].rearrange("p (n l) -> p n l", l=L), ALU.mult).then_inc(level_ready, 1)
                    else:
                        V_.tensor_copy(kl[lv % 2][:, :], k[:, CTX:ROWS]).then_inc(level_ready, 1)

                differences(0)
                factors(0)
                n = 0
                for lv in range(len(levels)):
                    if lv + 1 < len(levels):
                        differences(lv + 1)
                        factors(lv + 1)
                    for c in range(LT):
                        ve.wait_ge(scored, START + n + 1)
                        if lv:
                            ve.wait_ge(picked, START + n - LT + 1)
                        m = mk[:, lv, :].unsqueeze(1).broadcast_to([128, G_HEADS, CH])
                        V_.copy_predicated(A[:, c, :, :], m, pa[n % 2][:, :, :]).then_inc(picked, 1)
                        n += 1
                ve.wait_ge(ends_exp, START + 3)
                outs = 0
                for i, c in enumerate(order):
                    ve.wait_ge(turned, START + i + 1)
                    if i >= 2:
                        ve.wait_ge(updated, START + i - 1)
                    V_.tensor_copy(kbT[i % 2][:, :], pk[:, 0:128]).then_inc(turn_taken, 1)
                    ve.wait_ge(updated, START + i + 1)
                    ve.wait_ge(state, START + 1 + 2 * i)
                    V_.tensor_tensor(um[:, :], pu[:, 0:W], bm[:, :], ALU.mult).then_inc(state, 1)
                    ve.wait_ge(state, START + 2 + 2 * i)
                    if c >= first:
                        ve.wait_ge(mixed, START + outs + 1)
                        if outs >= 2:
                            ve.wait_ge(stored, START + 16 * (outs - 1))
                        V_.tensor_copy(o[outs % 2][:, :], po_[:, 0:W]).then_inc(out_taken, 1)
                        outs += 1
                    V_.scalar_tensor_tensor(S[:, :], S[:, :], decay[:, c:c + 1], um[:, :], ALU.mult, ALU.add).then_inc(state, 1)


def combine_second(nc, name, OD, OGF, OGB, P2, lam, g_sub, g_out, mix):
    B = 2
    AW, GW = A_HEADS * A_DV, G_HEADS * G_DV
    with Stage(nc, name) as st:
        sb, sem = st.sb, st.sem
        lm = sb("lm", [128, 4, A_DK])
        lp = sb("lp", [128, 2, A_DK])
        ls = sb("ls", [128, 2])
        nl = sb("nl", [128, 1])
        gs = sb("gs", [128, A_DV])
        go = sb("go", [128, G_DV])
        od = [sb(f"od{j}", [128, A_HEADS, 2, A_DV]) for j in range(B)]
        of = [sb(f"of{j}", [128, GW]) for j in range(B)]
        ob = [sb(f"ob{j}", [128, GW]) for j in range(B)]
        rg = [sb(f"rg{j}", [128, GW]) for j in range(B)]
        sg = [sb(f"sg{j}", [128, GW]) for j in range(B)]
        d = [sb(f"d{j}", [128, A_HEADS, A_DV]) for j in range(B)]
        sq = [sb(f"sq{j}", [128, AW]) for j in range(B)]
        s8 = [sb(f"s8_{j}", [128, 8]) for j in range(B)]
        out = [sb(f"out{j}", [128, AW + GW]) for j in range(B)]
        const_in, lam_step, lam_exp = sem("const_in"), sem("lam_step"), sem("lam_exp")
        t_in, steps, roots, sig, stored = ([sem(f"{n}{j}") for j in range(B)] for n in ("t_in", "steps", "roots", "sig", "stored"))
        passed_sp, passed_ve = sem("passed_sp"), sem("passed_ve")
        N = 17
        with nc.Block() as block:
            @block.sync
            def _(sp):
                st.open(sp)
                sp.dma_start(lm[:, :, :], lam.rearrange("a n -> (a n)").partition_broadcast(128)).then_inc(const_in, 16)
                sp.dma_start(gs[:, :], g_sub.partition_broadcast(128)).then_inc(const_in, 16)
                sp.dma_start(go[:, :], g_out.partition_broadcast(128)).then_inc(const_in, 16)
                with sp.Fori(0, LAT_TILES // B) as i:
                    for j in range(B):
                        row = (i * B + j) * 128 + CTX
                        wait_alone(sp, steps[j], START + i * N, passed_sp)
                        sp.dma_start(od[j][:, :, :, :], OD[bass.ds(row, 128), :]).then_inc(t_in[j], 16)
                        sp.dma_start(of[j][:, :], OGF[bass.ds(row, 128), :]).then_inc(t_in[j], 16)
                        sp.dma_start(ob[j][:, :], OGB[bass.ds(row, 128), :]).then_inc(t_in[j], 16)
                        sp.dma_start(rg[j][:, :], P2[bass.ds(row, 128), I_RB:I_GB]).then_inc(t_in[j], 16)
                    for j in range(B):
                        row = (i * B + j) * 128 + CTX
                        wait_alone(sp, steps[j], START + (i + 1) * N, passed_sp)
                        sp.dma_start(mix[bass.ds(row, 128), 0:AW + GW], out[j][:, :]).then_inc(stored[j], 16)
                for j in range(B):
                    sp.wait_ge(stored[j], START + LAT_TILES // B * 16)

            @block.scalar
            def _(act):
                act.wait_ge(lam_step, START + 2)
                nc.scalar.activation(ls[:, :], ls[:, :], ACT.Exp).then_inc(lam_exp, 1)
                with act.Fori(0, LAT_TILES // B) as i:
                    for j in range(B):
                        act.wait_ge(t_in[j], START + (i + 1) * 64)
                        act.wait_ge(steps[j], START + i * N)
                        nc.scalar.activation(sg[j][:, :], rg[j][:, :], ACT.Exp, scale=-1.0).then_inc(sig[j], 1)
                        act.wait_ge(steps[j], START + i * N + 9)
                        nc.scalar.activation(s8[j][:, :], s8[j][:, :], ACT.Sqrt).then_inc(roots[j], 1)

            @block.vector
            def _(ve):
                V_ = nc.vector
                ve.wait_ge(const_in, START + 48)
                V_.tensor_tensor(lp[:, :, :], lm[:, 0:4:2, :], lm[:, 1:4:2, :], ALU.mult).then_inc(lam_step, 1)
                ve.wait_ge(lam_step, START + 1)
                V_.tensor_reduce(ls[:, :], lp[:, :, :], AX.X, ALU.add).then_inc(lam_step, 1)
                ve.wait_ge(lam_exp, START + 1)
                V_.tensor_scalar(nl[:, :], ls[:, 1:2], ls[:, 0:1], None, ALU.subtract).then_inc(lam_step, 1)
                ve.wait_ge(lam_step, START + 3)
                V_.tensor_scalar(nl[:, :], nl[:, :], -LAMBDA_START, None, ALU.add).then_inc(lam_step, 1)
                ve.wait_ge(lam_step, START + 4)
                with ve.Fori(0, LAT_TILES // B) as i:
                    for j in range(B):
                        count = [0]

                        def step(ins):
                            count[0] += 1
                            ins.then_inc(steps[j], 1)
                            ve.wait_ge(steps[j], START + i * N + count[0])

                        wait_alone(ve, t_in[j], START + (i + 1) * 64, passed_ve)
                        wait_alone(ve, stored[j], START + i * 16, passed_ve)
                        step(V_.scalar_tensor_tensor(d[j][:, :, :], od[j][:, :, 1, :], nl[:, 0:1], od[j][:, :, 0, :], ALU.mult, ALU.add))
                        step(V_.tensor_tensor(of[j][:, :], of[j][:, :], ob[j][:, :], ALU.add))
                        step(V_.tensor_tensor(sq[j][:, :], d[j][:, :, :].rearrange("p h d -> p (h d)"), d[j][:, :, :].rearrange("p h d -> p (h d)"), ALU.mult))
                        step(V_.tensor_reduce(s8[j][:, 0:4], sq[j][:, :].rearrange("p (h d) -> p h d", d=A_DV), AX.X, ALU.add))
                        step(V_.tensor_tensor(sq[j][:, 0:GW], of[j][:, :], of[j][:, :], ALU.mult))
                        step(V_.tensor_reduce(s8[j][:, 4:8], sq[j][:, 0:GW].rearrange("p (h d) -> p h d", d=G_DV), AX.X, ALU.add))
                        step(V_.tensor_scalar(s8[j][:, 0:4], s8[j][:, 0:4], 1.0 / A_DV, EPS, ALU.mult, ALU.add))
                        step(V_.tensor_scalar(s8[j][:, 4:8], s8[j][:, 4:8], 1.0 / G_DV, EPS, ALU.mult, ALU.add))
                        wait_alone(ve, sig[j], START + i + 1, passed_ve)
                        step(V_.tensor_scalar(sg[j][:, :], sg[j][:, :], 1.0, None, ALU.add))
                        step(V_.reciprocal(sg[j][:, :], sg[j][:, :]))
                        step(V_.tensor_tensor(rg[j][:, :], rg[j][:, :], sg[j][:, :], ALU.mult))
                        wait_alone(ve, roots[j], START + i + 1, passed_ve)
                        step(V_.reciprocal(s8[j][:, :], s8[j][:, :]))
                        ra = s8[j][:, 0:4].unsqueeze(2).broadcast_to([128, A_HEADS, A_DV])
                        rb = s8[j][:, 4:8].unsqueeze(2).broadcast_to([128, G_HEADS, G_DV])
                        step(V_.scalar_tensor_tensor(d[j][:, :, :], d[j][:, :, :], 1.0 - LAMBDA_START, ra, ALU.mult, ALU.mult))
                        ga = gs[:, :].unsqueeze(1).broadcast_to([128, A_HEADS, A_DV])
                        gb = go[:, :].unsqueeze(1).broadcast_to([128, G_HEADS, G_DV])
                        step(V_.tensor_tensor(out[j][:, 0:AW].rearrange("p (h d) -> p h d", d=A_DV), d[j][:, :, :], ga, ALU.mult))
                        o3 = of[j][:, :].rearrange("p (h d) -> p h d", d=G_DV)
                        step(V_.tensor_tensor(o3, o3, rb, ALU.mult))
                        step(V_.tensor_tensor(o3, o3, gb, ALU.mult))
                        step(V_.tensor_tensor(out[j][:, AW:], of[j][:, :], rg[j][:, :], ALU.mult))
                        assert count[0] == N


N_GROUPS, PER_GROUP = 4, 8
N_EXP = N_GROUPS * PER_GROUP
TOP = 2
MAX_BLOCKS = (SEQ * TOP + N_EXP * 127) // 128
MAX_BLOCKS += MAX_BLOCKS % 2
SURE_BLOCKS = SEQ * TOP // 128


def dispatch(nc, name, X, cols_a, cols_b, w_group, b_group, w_expert, b_expert, consts, XN, SLOTS, dest, gate, table, identity):
    NL = N_GROUPS + N_EXP
    T = LAT_TILES
    B = 2
    with Stage(nc, name) as st:
        sb, ps, sem = st.sb, st.ps, st.sem
        rw = sb("rw", [128, KD, NL])
        rb = sb("rb", [128, NL])
        cst = sb("cst", [128, consts.shape[1]])
        before, ones = cst[:, 0:128], cst[:, 128:256]
        number = cst[:, 256:256 + N_EXP]
        blocks = cst[:, 288:288 + MAX_BLOCKS]
        row_of = cst[:, 336:336 + T]
        ssum = sb("ssum", [128, T])
        junk = sb("junk", [128, D])
        xn = [sb(f"xn{j}", [128, D]) for j in range(B)]
        hT = [sb(f"hT{j}", [128, KD, 128]) for j in range(B)]
        lg = sb("lg", [128, T, NL])
        gmax, gsum, rest, e1 = sb("gmax", [128, T]), sb("gsum", [128, T]), sb("rest", [128, T]), sb("e1", [128, T])
        gexp = sb("gexp", [128, T, N_GROUPS])
        pick = sb("pick", [128, T, N_GROUPS])
        low = sb("low", [128, T, N_GROUPS])
        em = sb("em", [128, T, N_EXP])
        top8 = sb("top8", [128, T, 8])
        at8 = sb("at8", [128, T, 8], u32)
        atf = sb("atf", [128, TOP, T])
        hot = [sb(f"hot{s}", [128, T, N_EXP]) for s in range(TOP)]
        both = sb("both", [128, T, N_EXP])
        upto = sb("upto", [128, T + 1, N_EXP])
        nb, pend, pstart, onesr = sb("nb", [128, N_EXP]), sb("pend", [128, N_EXP]), sb("pstart", [128, N_EXP]), sb("onesr", [128, N_EXP])
        place = sb("place", [128, T, N_EXP])
        prod = sb("prod", [128, T, N_EXP])
        destf = sb("destf", [128, TOP, T])
        cmp = sb("cmp", [128, MAX_BLOCKS, N_EXP])
        tabf = sb("tabf", [128, MAX_BLOCKS + 1])
        halfc = sb("halfc", [128, MAX_BLOCKS // 2])
        row_i = sb("row_i", [128, T], i32)
        fill = sb("fill", [128, MAX_BLOCKS], i32)
        turnedP = [ps(f"turned{j}", [128, KD, 128]) for j in range(B)]
        logits = [ps(f"logits{j}", [128, 512]) for j in range(B)]
        pref = ps("pref", [128, T, N_EXP])
        cnt = ps("cnt", [128, 512])
        w_in, squares, mean, root, inv = sem("w_in"), sem("squares"), sem("mean"), sem("root"), sem("inv")
        normed, stored, turned, h_ready, scored, logged = ([sem(f"{n}{j}") for j in range(B)] for n in
                                                           ("normed", "stored", "turned", "h_ready", "scored", "logged"))
        steps, exps, counted, filled = sem("steps"), sem("exps"), sem("counted"), sem("filled")
        scattered = sem("scattered", from_zero=True)
        passed_sp, passed_ve, passed_act = sem("passed_sp"), sem("passed_ve"), sem("passed_act")
        marks = {}
        with nc.Block() as block:
            @block.vector
            def _(ve):
                V_ = nc.vector
                ve.wait_ge(squares, START + T)
                V_.tensor_scalar(ssum[:, :], ssum[:, :], 1.0 / D, EPS, ALU.mult, ALU.add).then_inc(mean, 1)
                ve.wait_ge(root, START + 1)
                V_.reciprocal(ssum[:, :], ssum[:, :]).then_inc(inv, 1)
                ve.wait_ge(w_in, START + 80)
                with ve.Fori(0, T // B) as i:
                    for j in range(B):
                        wait_alone(ve, turned[j], START + i + 1, passed_ve)
                        wait_alone(ve, scored[j], START + i, passed_ve)
                        for k in range(KD):
                            V_.tensor_scalar(hT[j][:, k, :], turnedP[j][:, k, :], cols_a[:, k, 0:1], cols_b[:, k, 0:1],
                                             ALU.mult, ALU.add).then_inc(h_ready[j], 1)
                    for j in range(B):
                        wait_alone(ve, scored[j], START + i + 1, passed_ve)
                        V_.tensor_tensor(lg[:, bass.ds(i * B + j, 1), :].rearrange("p a n -> p (a n)"), logits[j][:, 0:NL], rb[:, :], ALU.add).then_inc(logged[j], 1)
                for j in range(B):
                    ve.wait_ge(logged[j], START + T // B)
                count = [0]

                def step(ins):
                    count[0] += 1
                    ins.then_inc(steps, 1)
                    ve.wait_ge(steps, START + count[0])

                g = lg[:, :, 0:N_GROUPS]
                step(V_.tensor_reduce(gmax[:, :], g, AX.X, ALU.max))
                gm = gmax[:, :].unsqueeze(2).broadcast_to([128, T, N_GROUPS])
                step(V_.tensor_tensor(gexp[:, :, :], g, gm, ALU.subtract))
                marks["group_differences"] = count[0]
                step(V_.tensor_tensor(pick[:, :, :], g, gm, ALU.is_equal))
                step(V_.memset(rest[:, :], 1.0))
                for q in range(N_GROUPS):
                    step(V_.tensor_tensor(pick[:, :, q], pick[:, :, q], rest[:, :], ALU.mult))
                    step(V_.tensor_tensor(rest[:, :], rest[:, :], pick[:, :, q], ALU.subtract))
                step(V_.tensor_scalar(low[:, :, :], pick[:, :, :], -NEG, NEG, ALU.mult, ALU.add))
                e4 = lg[:, :, N_GROUPS:NL].rearrange("p t (g e) -> p t g e", e=PER_GROUP)
                l4 = low[:, :, :].unsqueeze(3).broadcast_to([128, T, N_GROUPS, PER_GROUP])
                for t in range(T):
                    step(V_.tensor_tensor(em[:, t, :].rearrange("p (g e) -> p g e", e=PER_GROUP), e4[:, t, :, :], l4[:, t, :, :], ALU.add))
                    step(V_.max(top8[:, t, :], em[:, t, :]))
                    step(V_.max_index(at8[:, t, :], top8[:, t, :], em[:, t, :]))
                for s in range(TOP):
                    step(V_.tensor_copy(atf[:, s, :], at8[:, :, s]))
                step(V_.tensor_tensor(e1[:, :], top8[:, :, 1], top8[:, :, 0], ALU.subtract))
                marks["expert_differences"] = count[0]
                for s in range(TOP):
                    step(V_.tensor_tensor(hot[s][:, :, :], number.unsqueeze(1).broadcast_to([128, T, N_EXP]),
                                          atf[:, s, :].unsqueeze(2).broadcast_to([128, T, N_EXP]), ALU.is_equal))
                step(V_.tensor_tensor(both[:, :, :], hot[0][:, :, :], hot[1][:, :, :], ALU.add))
                step(V_.memset(upto[:, 0, :], 0.0))
                for t in range(T):
                    step(V_.tensor_tensor(upto[:, t + 1, :], upto[:, t, :], both[:, t, :], ALU.add))
                marks["sums"] = count[0]
                ve.wait_ge(exps, START + 2)
                step(V_.tensor_reduce(gsum[:, :], gexp[:, :, :], AX.X, ALU.add))
                step(V_.reciprocal(gsum[:, :], gsum[:, :]))
                step(V_.tensor_scalar(rest[:, :], e1[:, :], 1.0, None, ALU.add))
                step(V_.reciprocal(rest[:, :], rest[:, :]))
                step(V_.tensor_tensor(gate[:, 0, :], rest[:, :], gsum[:, :], ALU.mult))
                step(V_.tensor_tensor(gate[:, 1, :], gate[:, 0, :], e1[:, :], ALU.mult))
                ve.wait_ge(counted, START + 1)
                step(V_.tensor_scalar(nb[:, :], cnt[:, 0:N_EXP], 0.0, None, ALU.is_gt))
                for q in range(1, SEQ // 128):
                    step(V_.scalar_tensor_tensor(nb[:, :], cnt[:, 0:N_EXP], float(128 * q), nb[:, :], ALU.is_gt, ALU.add))
                step(V_.memset(onesr[:, :], 1.0))
                step(V_.tensor_tensor_scan(pend[:, :], onesr[:, :], nb[:, :], 0.0, ALU.mult, ALU.add))
                step(V_.tensor_tensor(pstart[:, :], pend[:, :], nb[:, :], ALU.subtract))
                step(V_.tensor_scalar(pstart[:, :], pstart[:, :], 128.0, None, ALU.mult))
                step(V_.tensor_tensor(place[:, :, :], pref[:, :, :], pstart[:, :].unsqueeze(1).broadcast_to([128, T, N_EXP]), ALU.add))
                for s in range(TOP):
                    step(V_.tensor_tensor(prod[:, :, :], place[:, :, :], hot[s][:, :, :], ALU.mult))
                    step(V_.tensor_reduce(destf[:, s, :], prod[:, :, :], AX.X, ALU.add))
                step(V_.tensor_copy(dest[:, :, :], destf[:, :, :]))
                step(V_.tensor_copy(row_i[:, :], row_of))
                marks["destinations"] = count[0]
                step(V_.tensor_tensor(cmp[:, :, :], pend[:, :].unsqueeze(1).broadcast_to([128, MAX_BLOCKS, N_EXP]),
                                      blocks.unsqueeze(2).broadcast_to([128, MAX_BLOCKS, N_EXP]), ALU.is_le))
                step(V_.tensor_reduce(tabf[:, 0:MAX_BLOCKS], cmp[:, :, :], AX.X, ALU.add))
                step(V_.tensor_scalar(tabf[:, 0:MAX_BLOCKS], tabf[:, 0:MAX_BLOCKS], float(N_EXP - 1), None, ALU.min))
                step(V_.tensor_scalar(halfc[:, :], blocks[:, 0:MAX_BLOCKS:2], pend[:, N_EXP - 1:N_EXP], None, ALU.is_lt))
                step(V_.tensor_reduce(tabf[:, MAX_BLOCKS:], halfc[:, :], AX.X, ALU.add))
                step(V_.tensor_copy(table[:, :], tabf[:, :]))

            @block.sync
            def _(sp):
                st.open(sp)
                sp.dma_start(rw[:, :, 0:N_GROUPS], w_group.rearrange("(k p) e -> p k e", p=128)).then_inc(w_in, 16)
                sp.dma_start(rw[:, :, N_GROUPS:NL], w_expert.rearrange("(k p) e -> p k e", p=128)).then_inc(w_in, 16)
                sp.dma_start(rb[:, 0:N_GROUPS], b_group.partition_broadcast(128)).then_inc(w_in, 16)
                sp.dma_start(rb[:, N_GROUPS:NL], b_expert.partition_broadcast(128)).then_inc(w_in, 16)
                sp.dma_start(cst[:, :], consts).then_inc(w_in, 16)
                with sp.Fori(0, T // B) as i:
                    for j in range(B):
                        wait_alone(sp, normed[j], START + i + 1, passed_sp)
                        sp.dma_start(XN[bass.ds((CTX_TILES + i * B + j) * 128, 128), :], xn[j][:, :]).then_inc(stored[j], 16)
                for j in range(B):
                    sp.wait_ge(stored[j], START + T // B * 16)

            @block.gpsimd
            def _(po):
                nc.gpsimd.memset(fill[:, :], CTX).then_inc(filled, 1)
                po.wait_ge(filled, START + 1)
                po.dma_start(SLOTS.rearrange("(p n) a -> p (n a)", n=MAX_BLOCKS), fill[:, :]).then_inc(scattered, 16)
                po.wait_ge(scattered, 16)
                po.wait_ge(steps, START + marks["destinations"])
                for s in range(TOP):
                    for t in range(T):
                        po.indirect_dma_start(SLOTS, bass.IndirectOffsetOnAxis(ap=dest[:, s, t:t + 1], axis=0), row_i[:, t:t + 1], None).then_inc(scattered, 16)
                po.wait_ge(scattered, 16 + 16 * TOP * T)

            @block.scalar
            def _(act):
                for t in range(T):
                    if t:
                        act.wait_ge(squares, START + t)
                    nc.scalar.activation(junk[:, :], X[:, CTX_TILES + t, :], ACT.Square, accum_out=ssum[:, t:t + 1]).then_inc(squares, 1)
                act.wait_ge(mean, START + 1)
                nc.scalar.activation(ssum[:, :], ssum[:, :], ACT.Sqrt).then_inc(root, 1)
                act.wait_ge(inv, START + 1)
                with act.Fori(0, T // B) as i:
                    for j in range(B):
                        act.wait_ge(stored[j], START + i * 16)
                        act.wait_ge(turned[j], START + i)
                        act.sem_inc(passed_act, 1)
                        nc.scalar.activation(xn[j][:, :], X[:, bass.ds(CTX_TILES + i * B + j, 1), :], ACT.Copy,
                                             scale=ssum[:, bass.ds(i * B + j, 1)]).then_inc(normed[j], 1)
                act.wait_ge(steps, START + marks["group_differences"])
                nc.scalar.activation(gexp[:, :, :], gexp[:, :, :], ACT.Exp).then_inc(exps, 1)
                act.wait_ge(steps, START + marks["expert_differences"])
                nc.scalar.activation(e1[:, :], e1[:, :], ACT.Exp).then_inc(exps, 1)

            @block.tensor
            def _(pe):
                pe.wait_ge(w_in, START + 80)
                with pe.Fori(0, T // B) as i:
                    for j in range(B):
                        pe.wait_ge(normed[j], START + i + 1)
                        pe.wait_ge(h_ready[j], START + i * KD)
                        for k in range(KD):
                            tp = nc.tensor.transpose(turnedP[j][:, k, :], xn[j][:, k * 128:(k + 1) * 128], identity[:, :])
                        tp.then_inc(turned[j], 1)
                    for j in range(B):
                        pe.wait_ge(h_ready[j], START + (i + 1) * KD)
                        pe.wait_ge(logged[j], START + i)
                        for k in range(KD):
                            mm = nc.tensor.matmul(logits[j][:, 0:NL], hT[j][:, k, :], rw[:, k, :], start=(k == 0), stop=(k == KD - 1))
                        mm.then_inc(scored[j], 1)
                pe.wait_ge(steps, START + marks["sums"])
                flat = pref[:, :, :].rearrange("p t e -> p (t e)")
                nc.tensor.matmul(flat, before, both[:, :, :].rearrange("p t e -> p (t e)"), start=True, stop=False)
                nc.tensor.matmul(flat, ones, upto[:, 0:T, :].rearrange("p t e -> p (t e)"), start=False, stop=True)
                nc.tensor.matmul(cnt[:, 0:N_EXP], ones, upto[:, T, :], start=True, stop=True).then_inc(counted, 1)


def block_experts(nc, name, XN, SLOTS, YB, table, cols_a, cols_b, w_up, w_down, identity):
    B = 2
    with Stage(nc, name) as st:
        sb, ps, sem = st.sb, st.ps, st.sem
        wu = [sb(f"wu{j}", [128, KD, 2 * FF]) for j in range(B)]
        wd = [sb(f"wd{j}", [128, KF, D]) for j in range(B)]
        idx = [sb(f"idx{j}", [128, 1], i32) for j in range(B)]
        xg = [sb(f"xg{j}", [128, D]) for j in range(B)]
        xT = sb("xT", [128, KD, 128])
        hid = sb("hid", [128, KF, 128])
        ex = [sb(f"ex{j}", [128, 128]) for j in range(2)]
        y = [sb(f"y{j}", [128, D]) for j in range(B)]
        turnedP = ps("turned", [128, KD, 128])
        gu = [ps(f"gu{j}", [128, 2, 128]) for j in range(2)]
        acc = [ps(f"acc{j}", [128, 512]) for j in range(4)]
        w_in, idx_in, down_done, stored = ([sem(f"{n}{j}") for j in range(B)] for n in ("w_in", "idx_in", "down_done", "stored"))
        gathered = [sem(f"gathered{j}", from_zero=True) for j in range(B)]
        turned, x_ready, upped, raised, steps, downed, y_ready, fetched = (sem(n) for n in ("turned", "x_ready", "upped", "raised", "steps", "downed", "y_ready", "fetched"))
        passed_sp, passed_ve, passed_po, passed_act = sem("passed_sp"), sem("passed_ve"), sem("passed_po"), sem("passed_act")
        with nc.Block() as block:
            @block.sync
            def _(sp):
                st.open(sp)
                pairs = sp.value_load(table[0:1, MAX_BLOCKS:MAX_BLOCKS + 1], min_val=1, max_val=MAX_BLOCKS // 2)
                with sp.Fori(0, pairs) as i:
                    for j in range(B):
                        b = i * B + j
                        wait_alone(sp, fetched, START + i * B, passed_sp)
                        sp.dma_start(idx[j][:, :], SLOTS[bass.ds(b * 128, 128), :]).then_inc(idx_in[j], 16)
                        e = sp.value_load(table[0:1, bass.ds(b, 1)], min_val=0, max_val=N_EXP - 1)
                        wait_alone(sp, down_done[j], START + i, passed_sp)
                        sp.dma_start(wu[j][:, :, :], w_up[bass.ds(e, 1), :, :].rearrange("e (k p) n -> p (e k) n", p=128)).then_inc(w_in[j], 16)
                        sp.dma_start(wd[j][:, :, :], w_down[bass.ds(e, 1), :, :].rearrange("e (k p) n -> p (e k) n", p=128)).then_inc(w_in[j], 16)

            @block.gpsimd
            def _(po):
                pairs = po.value_load(table[0:1, MAX_BLOCKS:MAX_BLOCKS + 1], min_val=1, max_val=MAX_BLOCKS // 2)
                with po.Fori(0, pairs) as i:
                    for j in range(B):
                        wait_alone(po, idx_in[j], START + (i + 1) * 16, passed_po)
                        wait_alone(po, turned, START + i * B, passed_po)
                        po.indirect_dma_start(xg[j][:, :], None, XN, bass.IndirectOffsetOnAxis(ap=idx[j][:, :], axis=0)).then_inc(gathered[j], 16)
                    for j in range(B):
                        wait_alone(po, gathered[j], (i + 1) * 16, fetched)

            @block.scalar
            def _(act):
                pairs = act.value_load(table[0:1, MAX_BLOCKS:MAX_BLOCKS + 1], min_val=1, max_val=MAX_BLOCKS // 2)
                with act.Fori(0, pairs) as i:
                    for j in range(B):
                        b = i * B + j
                        for f in range(KF):
                            act.wait_ge(upped, START + b * KF + f + 1)
                            act.wait_ge(steps, START + (b * KF + max(f - 1, 0)) * 4)
                            nc.scalar.activation(ex[f % 2][:, :], gu[f % 2][:, 0, :], ACT.Exp, scale=-1.0).then_inc(raised, 1)
                        for c in range(2):
                            act.wait_ge(downed, START + b * 2 + c + 1)
                            act.wait_ge(stored[j], START + i * 16)
                            nc.scalar.activation(y[j][:, c * 512:(c + 1) * 512], acc[2 * j + c][:, :], ACT.Copy).then_inc(y_ready, 1)
                        act.wait_ge(y_ready, START + (b + 1) * 2)
                        act.sem_inc(down_done[j], 1)
                        nc.scalar.dma_start(YB[bass.ds(b * 128, 128), :], y[j][:, :]).then_inc(stored[j], 16)
                for j in range(B):
                    wait_alone(act, stored[j], START + pairs * 16, passed_act)

            @block.tensor
            def _(pe):
                pairs = pe.value_load(table[0:1, MAX_BLOCKS:MAX_BLOCKS + 1], min_val=1, max_val=MAX_BLOCKS // 2)
                with pe.Fori(0, pairs) as i:
                    for j in range(B):
                        b = i * B + j
                        pe.wait_ge(gathered[j], (i + 1) * 16)
                        pe.wait_ge(x_ready, START + b * KD)
                        for k in range(KD):
                            tp = nc.tensor.transpose(turnedP[:, k, :], xg[j][:, k * 128:(k + 1) * 128], identity[:, :])
                        tp.then_inc(turned, 1)
                        pe.wait_ge(x_ready, START + (b + 1) * KD)
                        pe.wait_ge(w_in[j], START + (i + 1) * 32)
                        for f in range(KF):
                            pe.wait_ge(steps, START + (b * KF + max(f - 1, 0)) * 4)
                            for h in range(2):
                                for k in range(KD):
                                    mm = nc.tensor.matmul(gu[f % 2][:, h, :], wu[j][:, k, h * FF + f * 128:h * FF + (f + 1) * 128], xT[:, k, :],
                                                          start=(k == 0), stop=(k == KD - 1))
                            mm.then_inc(upped, 1)
                        pe.wait_ge(steps, START + (b + 1) * KF * 4)
                        pe.wait_ge(y_ready, START + i * B * 2)
                        for c in range(2):
                            for f in range(KF):
                                mm = nc.tensor.matmul(acc[2 * j + c][:, :], hid[:, f, :], wd[j][:, f, c * 512:(c + 1) * 512], start=(f == 0), stop=(f == KF - 1))
                            mm.then_inc(downed, 1)

            @block.vector
            def _(ve):
                pairs = ve.value_load(table[0:1, MAX_BLOCKS:MAX_BLOCKS + 1], min_val=1, max_val=MAX_BLOCKS // 2)
                with ve.Fori(0, pairs) as i:
                    for j in range(B):
                        b = i * B + j
                        wait_alone(ve, turned, START + b + 1, passed_ve)
                        wait_alone(ve, upped, START + b * KF, passed_ve)
                        for k in range(KD):
                            nc.vector.tensor_scalar(xT[:, k, :], turnedP[:, k, :], cols_a[:, k, 0:1], cols_b[:, k, 0:1], ALU.mult, ALU.add).then_inc(x_ready, 1)
                        for f in range(KF):
                            base = (b * KF + f) * 4
                            wait_alone(ve, raised, START + b * KF + f + 1, passed_ve)
                            wait_alone(ve, downed, START + b * 2, passed_ve)
                            nc.vector.tensor_scalar(ex[f % 2][:, :], ex[f % 2][:, :], 1.0, None, ALU.add).then_inc(steps, 1)
                            wait_alone(ve, steps, START + base + 1, passed_ve)
                            nc.vector.reciprocal(ex[f % 2][:, :], ex[f % 2][:, :]).then_inc(steps, 1)
                            wait_alone(ve, steps, START + base + 2, passed_ve)
                            nc.vector.tensor_tensor(ex[f % 2][:, :], ex[f % 2][:, :], gu[f % 2][:, 0, :], ALU.mult).then_inc(steps, 1)
                            wait_alone(ve, steps, START + base + 3, passed_ve)
                            nc.vector.tensor_tensor(hid[:, f, :], ex[f % 2][:, :], gu[f % 2][:, 1, :], ALU.mult).then_inc(steps, 1)


def collect(nc, name, YB, dest, gate, out_gate, X):
    T = LAT_TILES
    with Stage(nc, name) as st:
        sb, sem = st.sb, st.sem
        og = sb("og", [128, D])
        y = [[sb(f"y{j}_{s}", [128, D]) for s in range(TOP)] for j in range(2)]
        g_in, steps = sem("g_in"), sem("steps")
        got = [sem(f"got{t}", from_zero=True) for t in range(T)]
        with nc.Block() as block:
            @block.sync
            def _(sp):
                st.open(sp)
                sp.dma_start(og[:, :], out_gate.partition_broadcast(128)).then_inc(g_in, 16)

            @block.gpsimd
            def _(po):
                for t in range(T):
                    if t >= 2:
                        po.wait_ge(steps, START + 4 * (t - 1))
                    for s in range(TOP):
                        po.indirect_dma_start(y[t % 2][s][:, :], None, YB, bass.IndirectOffsetOnAxis(ap=dest[:, s, t:t + 1], axis=0)).then_inc(got[t], 16)

            @block.vector
            def _(ve):
                ve.wait_ge(g_in, START + 16)
                for t in range(T):
                    a, b = y[t % 2]
                    ve.wait_ge(got[t], 32)
                    nc.vector.tensor_scalar(a[:, :], a[:, :], gate[:, 0, t:t + 1], None, ALU.mult).then_inc(steps, 1)
                    ve.wait_ge(steps, START + 4 * t + 1)
                    nc.vector.scalar_tensor_tensor(a[:, :], b[:, :], gate[:, 1, t:t + 1], a[:, :], ALU.mult, ALU.add).then_inc(steps, 1)
                    ve.wait_ge(steps, START + 4 * t + 2)
                    nc.vector.tensor_tensor(a[:, :], a[:, :], og[:, :], ALU.mult).then_inc(steps, 1)
                    ve.wait_ge(steps, START + 4 * t + 3)
                    xt = X[:, CTX_TILES + t, :]
                    nc.vector.tensor_tensor(xt, xt, a[:, :], ALU.add).then_inc(steps, 1)
                ve.wait_ge(steps, START + 4 * T)


def _rope_table():
    import numpy as np
    out = []
    for rot in (32, 64):
        n_freq = rot // 4
        t = np.arange(SEQ)
        inv = np.float32(10000.0) ** (-np.arange(n_freq, dtype=np.float32) / np.float32(n_freq))
        ang = np.concatenate([(t // 64).astype(np.float32)[:, None] * inv, (t % 64).astype(np.float32)[:, None] * inv], -1)
        cos = np.concatenate([np.ones((CTX, rot // 2)), np.cos(ang)]).astype(np.float32)
        sin = np.concatenate([np.zeros((CTX, rot // 2)), np.sin(ang)]).astype(np.float32)
        out += [cos, cos, -sin, sin]
    return np.concatenate(out, -1).astype(np.float32)


def _window_masks():
    import numpy as np
    q = np.arange(128)[:, None]
    k = np.arange(384)[None, :] - 128
    return np.where(np.abs(q - k) <= 128, 0.0, NEG).astype(np.float32)


def _grid_rope_table():
    import numpy as np
    t = np.arange(SEQ)
    inv = np.float32(10000.0) ** (-np.arange(16, dtype=np.float32) / np.float32(16))
    ar = (t // GRID).astype(np.float32)[:, None] * inv
    ac = (t % GRID).astype(np.float32)[:, None] * inv
    lat = np.concatenate([np.cos(ar), np.cos(ar), np.cos(ac), np.cos(ac), -np.sin(ar), np.sin(ar), -np.sin(ac), np.sin(ac)], -1)
    ctx = np.concatenate([np.ones((CTX, 64)), np.zeros((CTX, 64))], -1)
    return np.concatenate([ctx, lat]).astype(np.float32)


def _neighbourhood_masks():
    import numpy as np
    rows = SEQ // GRID
    out = []
    for t in (0, 1, 2, 6, 7):
        start = min(max(2 * t - 4, 0), rows - 10)
        m = np.full((2, GRID, 10, GRID), NEG, np.float32)
        for a in range(2):
            r0 = min(max(2 * t + a - N_ROWS // 2, 0), rows - N_ROWS)
            for c in range(GRID):
                c0 = min(max(c - N_COLS // 2, 0), GRID - N_COLS)
                m[a, c, r0 - start:r0 - start + N_ROWS, c0:c0 + N_COLS] = 0.0
        out.append(m.reshape(128, BAND))
    return np.concatenate(out, -1)


def _level_masks(backward):
    import numpy as np
    s = np.arange(128)[:, None]
    t = np.arange(128)[None, :]
    if backward:
        s, t = 127 - s, 127 - t
    out = [(s // (2 * L) == t // (2 * L)) & (s % (2 * L) < L) & (t % (2 * L) >= L) for L in (64, 32, 16, 8, 4, 2, 1)]
    out.append(s == t)
    return np.stack(out, 1).astype(np.int32)


def _head_blocks():
    import numpy as np
    return (np.arange(128)[:, None] // G_DK == np.arange(256)[None, :] // G_DV).astype(np.float32)


def _routing_constants():
    import numpy as np
    p = np.arange(128)[:, None]
    before = (p < np.arange(128)[None, :])
    ones = np.ones((128, 128))
    experts = np.broadcast_to(np.arange(N_EXP)[None, :], (128, N_EXP))
    blocks = np.broadcast_to(np.arange(MAX_BLOCKS)[None, :], (128, MAX_BLOCKS))
    rows = p + 128 * np.arange(LAT_TILES)[None, :] + CTX
    return np.concatenate([before, ones, experts, blocks, rows], -1).astype(np.float32)


CONSTANTS = {"routing": _routing_constants, "rope2": _grid_rope_table, "near": _neighbourhood_masks, "levels_f": lambda: _level_masks(False),
             "levels_b": lambda: _level_masks(True), "head_blocks": _head_blocks, "window": _window_masks, "rope1": _rope_table}


def second_mixers(nc, t, X, identity, scratch, cols):
    gates, P2, RT2, OD, OGF, OGB, BT, padded, mix2 = (scratch[n] for n in ("gates", "P2", "RT2", "OD", "OGF", "OGB", "BT", "padded", "mix2"))
    modulation(nc, "m2", t["c_2"][0], t["c_ctx_2"], t["w_mod_2"][0], t["b_mod_2"][0], t["norm1_g_2"][0], t["norm2_g_2"][0], cols, gates, identity,
               lambda st: neighbourhood_bias(nc, st, t["na_rel_bias_2"][0], t["near"], padded, BT))
    project(nc, "p2", X, cols[:, 0, :, :], cols[:, 1, :, :], t["w_in_2"][0], IN2, 512, P2, identity)
    heads_second(nc, "h2", P2, t["rope2"], RT2, identity)
    diff_attention(nc, "da", RT2, P2, OD, identity)
    neighbourhood_attention(nc, "na", RT2, P2, BT, mix2, identity)
    for backward, OG, masks in ((False, OGF, t["levels_f"]), (True, OGB, t["levels_b"])):
        half = range(SURE_BLOCKS, MAX_BLOCKS)[int(backward)::2]
        blank = [scratch["YB"][b * 128:(b + 1) * 128, :] for b in half]
        gated_scan(nc, "gb" if backward else "gf", backward, RT2, P2, t["gla_w_decay_2"][0], t["gla_b_decay_2"][0], masks, t["head_blocks"], OG, blank, identity)
    combine_second(nc, "cb", OD, OGF, OGB, P2, t["diff_lambda_2"][0], t["diff_sub_g_2"][0], t["gla_norm_g_2"][0], mix2)


SECOND_SCRATCH = {"P2": [ROWS, IN2], "RT2": [R2, ROWS], "OD": [ROWS, 2 * A_HEADS * A_DV], "OGF": [ROWS, 256], "OGB": [ROWS, 256],
                  "BT": [N_HEADS, 128, PATTERNS * BAND], "padded": [GRID, N_HEADS, 19, 127]}
_SECOND = ["c_2", "c_ctx_2", "w_mod_2", "b_mod_2", "norm1_g_2", "norm2_g_2", "w_in_2", "diff_lambda_2", "diff_sub_g_2", "gla_w_decay_2",
           "gla_b_decay_2", "gla_norm_g_2", "na_rel_bias_2", "rope2", "near", "levels_f", "levels_b", "head_blocks"]


def second_block(nc, t, X, identity, scratch, out):
    with ExitStack() as own:
        def keep(name, shape, dt=fp32):
            return own.enter_context(nc.sbuf_tensor(name, shape, dt))

        cols = keep("cols2", [128, 4, KD, 2])
        second_mixers(nc, t, X, identity, scratch, cols)
        gates = scratch["gates"]
        mix_out(nc, "out2", CTX_TILES, LAT_TILES, scratch["mix2"], t["w_out_2"][0], gates[0, 2 * D:3 * D], X, identity)
        dest, gate, table = keep("dest", [128, TOP, LAT_TILES], i32), keep("gate", [128, TOP, LAT_TILES]), keep("table", [128, MAX_BLOCKS + 1], i32)
        a2, b2 = cols[:, 2, :, :], cols[:, 3, :, :]
        dispatch(nc, "disp", X, a2, b2, t["w_router_group_2"][0], t["b_router_group_2"][0], t["w_router_expert_2"][0],
                 t["b_router_expert_2"][0], t["routing"], scratch["XN"], scratch["SLOTS"], dest, gate, table, identity)
        block_experts(nc, "bexp", scratch["XN"], scratch["SLOTS"], scratch["YB"], table, a2, b2, t["w_expert_up_2"][0], t["w_expert_down_2"][0], identity)
        collect(nc, "coll", scratch["YB"], dest, gate, gates[0, 5 * D:6 * D], X)
        final_norm(nc, "final2", X, t["final_g_2"], out)


SCRATCH = {"gates": [2, 6 * D], "P1": [ROWS, IN1], "RT": [R1, ROWS], "V": [ROWS, M_HEADS * M_V], "Z": [ZROWS, CONV],
           "mix": [ROWS, M_HEADS * M_V + S_HEADS * S_DK], "XN": [ROWS, D], "F": [ROWS, D], "mix2": [ROWS, D], "YB": [MAX_BLOCKS * 128, D],
           **SECOND_SCRATCH}
_FIRST = ["x", "ctx", "c", "c_ctx", "ada_w", "ada_b", "norm1_g", "norm2_g", "w_in", "mla_w_uq", "mla_w_ukv", "mla_q_norm_g", "mla_kv_norm_g",
          "swa_sink", "conv_w", "w_o", "router_w", "exp_w_gate", "exp_w_up", "exp_w_down", "final_norm_g", "rope1", "window"]
_SECOND += ["ctx_2", "w_out_2", "norm2_g_2", "w_router_group_2", "b_router_group_2", "w_router_expert_2", "b_router_expert_2", "w_expert_up_2", "w_expert_down_2",
            "final_g_2", "routing"]
_SECOND = list(dict.fromkeys(_SECOND))


DEPTH = 2


def program(nc, t, out):
    ctx = ExitStack()
    with ctx:
        X = ctx.enter_context(nc.sbuf_tensor("X", [128, TILES, D], fp32))
        identity = ctx.enter_context(nc.sbuf_tensor("identity", [128, 128], fp32))
        scratch = {n: nc.dram_tensor(n, s, fp32).ap() for n, s in SCRATCH.items()}
        scratch["SLOTS"] = nc.dram_tensor("SLOTS", [MAX_BLOCKS * 128, 1], i32).ap()
        setup(nc, X, identity, t["x"][0], t["ctx"][0])
        first_block(nc, t, X, identity, scratch)
        final_norm(nc, "final1", X, t["final_norm_g"])
        next_context(nc, X, t["ctx_2"][0])
        second_block(nc, t, X, identity, scratch, out[0])


_INS = _FIRST + _SECOND
_OUTS = [((1, 1024, 1024), "float32")]


def kernel(**inputs):
    import numpy as _np
    import concourse.bacc as _bacc
    from concourse import mybir as _mybir
    from concourse.bass_utils import run_bass_kernel_spmd as _run

    nc = _bacc.Bacc("TRN2", target_bir_lowering=False, num_devices=1)
    arrays, args = {}, {}
    for name in _INS:
        a = _np.ascontiguousarray(inputs[name] if name in inputs else CONSTANTS[name]())
        arrays[f"in_{name}"] = a
        args[name] = nc.dram_tensor(f"in_{name}", a.shape, _mybir.dt.from_np(a.dtype), kind="ExternalInput").ap()
    outs = [nc.dram_tensor(f"out_{i}", shape, _mybir.dt.from_np(_np.dtype(dtype)), kind="ExternalOutput").ap()
            for i, (shape, dtype) in enumerate(_OUTS)]
    program(nc, args, *outs)
    r = _run(nc, [arrays], core_ids=[0])
    got = tuple(r.results[0][f"out_{i}"] for i in range(len(_OUTS)))
    return got[0] if len(got) == 1 else got
```
